# Optimizing a Trainium2 kernel written in Bass

```python
import math
import jax, jax.numpy as jnp
from jax import lax
import numpy as np

D_MODEL = 1024
BATCH = 1
SEQ = 1024
DEPTH = 1
DEC_BATCH = 8
DEC_SEQ = 8
PAST_LEN = 512
PAGE_SIZE = 128

MIX_WIDTH = D_MODEL
POOL_WIDTH = MIX_WIDTH // 4
POOL_WINDOWS = (2, 4, 8, 16)
POOL_GROUPS = len(POOL_WINDOWS)
POOL_GW = POOL_WIDTH // POOL_GROUPS
POOL_STATE = max(POOL_WINDOWS) - 1
ATTN_WIDTH = MIX_WIDTH - POOL_WIDTH
HEAD_DIM = 64
N_HEADS = ATTN_WIDTH // HEAD_DIM
BRANCHES = ((128, 1), (512, 4), (2048, 16))
STEPS = BRANCHES[0][0] // BRANCHES[0][1]
ATTN_REACH = max(w for w, _ in BRANCHES)
MAX_DIL = max(d for _, d in BRANCHES)
BLOCK = STEPS
PROJ_WIDTH = POOL_WIDTH + 3 * ATTN_WIDTH
N_GROUPS = 4
EXPERTS_PER_GROUP = 8
EXPERT_FF = 256
TOP_K_INNER = 2
RMS_EPS = 1e-6

kernel_name = 'hymba_pool_dilated_alibi_hmoe_step'

def alibi_slopes():
    def geometric(n):
        start = 2.0 ** (-8.0 / n)
        return [start ** (i + 1) for i in range(n)]
    c = 2 ** int(math.floor(math.log2(N_HEADS)))
    s = geometric(c)
    if c < N_HEADS:
        s = s + geometric(2 * c)[0::2][: N_HEADS - c]
    return jnp.asarray(s, dtype=jnp.float32)

def rmsnorm(x, g):
    xf = x.astype(jnp.float32)
    y = xf * lax.rsqrt(jnp.mean(xf * xf, axis=-1, keepdims=True) + RMS_EPS)
    return (y * g.astype(jnp.float32)).astype(x.dtype)

def mix_in(x, g_mix, w_in):
    n, t, _ = x.shape
    proj = jnp.einsum('btd,dc->btc', rmsnorm(x, g_mix), w_in)
    u = proj[..., :POOL_WIDTH]
    qkv = proj[..., POOL_WIDTH:].reshape(n, t, 3, N_HEADS, HEAD_DIM)
    return u, qkv[:, :, 0], qkv[:, :, 1], qkv[:, :, 2]

def pool_mix(u_ext, w_pool, pool_scale, n_out):
    L = u_ext.shape[1]
    uf = u_ext.astype(jnp.float32)
    cs = jnp.pad(jnp.cumsum(uf, axis=1), ((0, 0), (1, 0), (0, 0)))
    rows = jnp.arange(L - n_out, L)
    hi = cs[:, rows + 1]
    x_tok = uf[:, rows]
    outs = []
    for g, w in enumerate(POOL_WINDOWS):
        sl = slice(g * POOL_GW, (g + 1) * POOL_GW)
        lo = jnp.maximum(rows + 1 - w, 0)
        cnt = (rows + 1 - lo).astype(jnp.float32)
        mean = (hi[..., sl] - cs[:, lo, sl]) / cnt[None, :, None]
        outs.append(jnp.einsum('ntc,cd->ntd', mean - x_tok[..., sl], w_pool[g].astype(jnp.float32)))
    return (jnp.concatenate(outs, axis=-1) * pool_scale.astype(jnp.float32)).astype(u_ext.dtype)

def merge_branches(outs, lses):
    w = jax.nn.softmax(jnp.stack(lses), axis=0)
    return jnp.einsum('i...h,i...he->...he', w, jnp.stack(outs))

def branch_banded(q, k, v, d, slopes):
    b, s_pad, h, e = q.shape
    n = s_pad // d
    nb = n // BLOCK

    def split(t):
        t = t.reshape(b, n, d, h, e).transpose(0, 2, 1, 3, 4)
        return t.reshape(b, d, nb, BLOCK, h, e)

    def with_prev(t):
        prev = jnp.concatenate([jnp.zeros_like(t[:, :, :1]), t[:, :, :-1]], axis=2)
        return jnp.concatenate([prev, t], axis=3)

    qb = split(q)
    kc = with_prev(split(k))
    vc = with_prev(split(v))
    scores = jnp.einsum('brnqhe,brnkhe->brnhqk', qb, kc).astype(jnp.float32) * (HEAD_DIM ** -0.5)
    qi = jnp.arange(BLOCK)[:, None]
    ki = jnp.arange(2 * BLOCK)[None, :]
    step = qi + BLOCK - ki
    band = (step >= 0) & (step <= STEPS)
    valid = band[None] & ((jnp.arange(nb)[:, None, None] > 0) | (ki[None] >= BLOCK))
    bias = -slopes[:, None, None] * (d * step).astype(jnp.float32)[None]
    scores = jnp.where(valid[None, None, :, None], scores + bias, -jnp.inf)
    m = jnp.max(scores, axis=-1, keepdims=True)
    p = jnp.exp(scores - m)
    l = jnp.sum(p, axis=-1)
    o = jnp.einsum('brnhqk,brnkhe->brnqhe', p, vc.astype(jnp.float32)) / jnp.swapaxes(l, -1, -2)[..., None]
    lse = jnp.swapaxes(m[..., 0] + jnp.log(l), -1, -2)
    o = o.reshape(b, d, n, h, e).transpose(0, 2, 1, 3, 4).reshape(b, s_pad, h, e)
    lse = lse.reshape(b, d, n, h).transpose(0, 2, 1, 3).reshape(b, s_pad, h)
    return o, lse

def dilated_attention_prompt(q, k, v, slopes):
    s = q.shape[1]
    span = BLOCK * MAX_DIL
    s_pad = -(-s // span) * span
    pad = ((0, 0), (0, s_pad - s), (0, 0), (0, 0))
    qp, kp, vp = jnp.pad(q, pad), jnp.pad(k, pad), jnp.pad(v, pad)
    outs, lses = [], []
    for _, d in BRANCHES:
        o, lse = branch_banded(qp, kp, vp, d, slopes)
        outs.append(o[:, :s])
        lses.append(lse[:, :s])
    return merge_branches(outs, lses).astype(q.dtype)

def dilated_attention_sample(q, k_ext, v_ext, slopes):
    t = q.shape[1]
    lk = k_ext.shape[1]
    q_loc = lk - t + jnp.arange(t)
    j = jnp.arange(STEPS + 1)
    outs, lses = [], []
    for _, d in BRANCHES:
        idx = q_loc[:, None] - d * j[None, :]
        valid = idx >= 0
        idx = jnp.maximum(idx, 0)
        kg = k_ext[:, idx]
        vg = v_ext[:, idx]
        scores = jnp.einsum('nthe,ntjhe->nthj', q, kg).astype(jnp.float32) * (HEAD_DIM ** -0.5)
        scores = scores - slopes[:, None] * (d * j).astype(jnp.float32)[None, :]
        scores = jnp.where(valid[None, :, None, :], scores, -jnp.inf)
        m = jnp.max(scores, axis=-1, keepdims=True)
        p = jnp.exp(scores - m)
        l = jnp.sum(p, axis=-1)
        o = jnp.einsum('nthj,ntjhe->nthe', p, vg.astype(jnp.float32)) / l[..., None]
        outs.append(o)
        lses.append(m[..., 0] + jnp.log(l))
    return merge_branches(outs, lses).astype(q.dtype)

def mix_out(pool_out, attn_out, w_out):
    n, t = pool_out.shape[:2]
    cat = jnp.concatenate([pool_out, attn_out.reshape(n, t, ATTN_WIDTH)], axis=-1)
    return jnp.einsum('btc,cd->btd', cat, w_out)

def hier_moe(x, w_rg, b_rg, w_re, b_re, w_gate, w_up, w_down):
    lg = jnp.einsum('btd,dg->btg', x, w_rg).astype(jnp.float32) + b_rg.astype(jnp.float32)
    pg = jax.nn.softmax(lg, axis=-1)
    g_top = jnp.argmax(lg, axis=-1)
    p_sel = jnp.take_along_axis(pg, g_top[..., None], axis=-1)
    le = jnp.einsum('btd,gde->btge', x, w_re).astype(jnp.float32) + b_re.astype(jnp.float32)
    le_sel = jnp.take_along_axis(le, g_top[..., None, None], axis=2)[..., 0, :]
    pe = jax.nn.softmax(le_sel, axis=-1)
    top_v, top_i = lax.top_k(pe, TOP_K_INNER)
    top_v = top_v / jnp.sum(top_v, axis=-1, keepdims=True)
    gate_e = jnp.sum(jax.nn.one_hot(top_i, EXPERTS_PER_GROUP, dtype=jnp.float32) * top_v[..., None], axis=-2)
    group_gate = jax.nn.one_hot(g_top, N_GROUPS, dtype=jnp.float32) * p_sel
    out = jnp.zeros(x.shape, jnp.float32)
    for g in range(N_GROUPS):
        hg = jax.nn.silu(jnp.einsum('btd,edf->btef', x, w_gate[g])) * jnp.einsum('btd,edf->btef', x, w_up[g])
        wg = (group_gate[..., g:g + 1] * gate_e).astype(hg.dtype)
        out = out + jnp.einsum('btef,efd->btd', hg * wg[..., None], w_down[g]).astype(jnp.float32)
    return out.astype(x.dtype)

def setup_inputs(seed: int = 0) -> dict:
    key = jax.random.key(seed)
    ks = jax.random.split(key, 20)
    f32 = jnp.float32

    def nrm(k, shape, scale):
        return jax.random.normal(k, shape, f32) * scale

    kv_keep = min(ATTN_REACH, PAST_LEN)
    G, E, F, D = N_GROUPS, EXPERTS_PER_GROUP, EXPERT_FF, D_MODEL
    return {
        'x_prompt': nrm(ks[0], (BATCH, SEQ, D), 1.0),
        'x_sample': nrm(ks[1], (DEC_BATCH, DEC_SEQ, D), 1.0),
        'cache_k': nrm(ks[2], (DEPTH, DEC_BATCH, kv_keep, N_HEADS, HEAD_DIM), 1.0),
        'cache_v': nrm(ks[3], (DEPTH, DEC_BATCH, kv_keep, N_HEADS, HEAD_DIM), 1.0),
        'state_pool': nrm(ks[4], (DEPTH, DEC_BATCH, POOL_STATE, POOL_WIDTH), 1.0),
        'g_mix': 1.0 + nrm(ks[5], (DEPTH, D), 0.02),
        'w_in': nrm(ks[6], (DEPTH, D, PROJ_WIDTH), D ** -0.5),
        'w_pool': nrm(ks[7], (DEPTH, POOL_GROUPS, POOL_GW, POOL_GW), POOL_GW ** -0.5),
        'pool_scale': 1.0 + nrm(ks[8], (DEPTH, POOL_WIDTH), 0.1),
        'w_out': nrm(ks[9], (DEPTH, MIX_WIDTH, D), MIX_WIDTH ** -0.5),
        'g_ffn': 1.0 + nrm(ks[10], (DEPTH, D), 0.02),
        'w_router_group': nrm(ks[11], (DEPTH, D, G), D ** -0.5),
        'b_router_group': nrm(ks[12], (DEPTH, G), 0.01),
        'w_router_expert': nrm(ks[13], (DEPTH, G, D, E), D ** -0.5),
        'b_router_expert': nrm(ks[14], (DEPTH, G, E), 0.01),
        'w_gate': nrm(ks[15], (DEPTH, G, E, D, F), D ** -0.5),
        'w_up': nrm(ks[16], (DEPTH, G, E, D, F), D ** -0.5),
        'w_down': nrm(ks[17], (DEPTH, G, E, F, D), F ** -0.5),
        'g_final': 1.0 + nrm(ks[18], (D,), 0.02),
    }

def reference(x_prompt, x_sample, cache_k, cache_v, state_pool, g_mix, w_in, w_pool, pool_scale,
              w_out, g_ffn, w_router_group, b_router_group, w_router_expert, b_router_expert,
              w_gate, w_up, w_down, g_final):
    slopes = alibi_slopes()
    hp, hs = x_prompt, x_sample
    seq = x_prompt.shape[1]
    keep = min(ATTN_REACH, seq)
    kp_l, vp_l, pp_l, ks_l, vs_l, ps_l = [], [], [], [], [], []
    for layer in range(DEPTH):
        moe_w = (w_router_group[layer], b_router_group[layer], w_router_expert[layer],
                 b_router_expert[layer], w_gate[layer], w_up[layer], w_down[layer])
        u, q, k, v = mix_in(hp, g_mix[layer], w_in[layer])
        attn = dilated_attention_prompt(q, k, v, slopes)
        pool = pool_mix(u, w_pool[layer], pool_scale[layer], seq)
        hp = hp + mix_out(pool, attn, w_out[layer])
        hp = hp + hier_moe(rmsnorm(hp, g_ffn[layer]), *moe_w)
        kp_l.append(k[:, seq - keep:])
        vp_l.append(v[:, seq - keep:])
        pp_l.append(u[:, seq - POOL_STATE:])
        u, q, k, v = mix_in(hs, g_mix[layer], w_in[layer])
        k_ext = jnp.concatenate([cache_k[layer].astype(k.dtype), k], axis=1)
        v_ext = jnp.concatenate([cache_v[layer].astype(v.dtype), v], axis=1)
        attn = dilated_attention_sample(q, k_ext, v_ext, slopes)
        u_ext = jnp.concatenate([state_pool[layer].astype(u.dtype), u], axis=1)
        pool = pool_mix(u_ext, w_pool[layer], pool_scale[layer], hs.shape[1])
        hs = hs + mix_out(pool, attn, w_out[layer])
        hs = hs + hier_moe(rmsnorm(hs, g_ffn[layer]), *moe_w)
        ks_l.append(k)
        vs_l.append(v)
        ps_l.append(u_ext[:, -POOL_STATE:])
    y_prompt = rmsnorm(hp, g_final)
    y_sample = rmsnorm(hs, g_final)
    return (y_prompt, y_sample, jnp.stack(kp_l), jnp.stack(vp_l), jnp.stack(pp_l),
            jnp.stack(ks_l), jnp.stack(vs_l), jnp.stack(ps_l))


_drawn_inputs = setup_inputs


def setup_inputs(seed=0):
    import zlib

    import numpy as np

    out = dict(_drawn_inputs(seed))
    spreads = {}
    factors = {'b_router_group': 3.005, 'b_router_expert': 4.119, 'g_final': 2.888}
    for name, (base, spread) in spreads.items():
        noise = np.random.default_rng([zlib.crc32(name.encode()), seed]).standard_normal(out[name].shape)
        drawn = base * np.exp(spread * noise) if base else spread * noise
        out[name] = __import__('jax').numpy.asarray(drawn.astype(out[name].dtype))
    for name, factor in factors.items():
        out[name] = (out[name] * factor).astype(out[name].dtype)
    return out
```

```python
from contextlib import ExitStack

import concourse.bass as bass
import numpy as np
from concourse import mybir

F32 = mybir.dt.float32
F32R = mybir.dt.float32r
I32 = mybir.dt.int32
U32 = mybir.dt.uint32
ALU = mybir.AluOpType
ACT = mybir.ActivationFunctionType
AX = mybir.AxisListType

P = 128
D = 1024
KD = D // P
SEQ = 1024
NSEQ, TDEC = 8, 8
SMP = NSEQ * TDEC
TOK = SEQ + SMP
QT = SEQ // P
NT = QT + 1
PAST = 512
HEADS, HD = 12, 64
PAIRS = HEADS // 2
POOLW = 256
ATTW = HEADS * HD
POOL_STATE = 15
WINDOWS = (2, 4, 8, 16)
GROUPS, EPG, FF = 4, 8, 256
EXPERTS = GROUPS * EPG
EPS = 1e-6
SCALE = HD ** -0.5
MASKED = -1e30
BIG = 3e38

CAP = 96
OVER = (2 * TOK) // CAP
RING = 4
JOBS = -(-(EXPERTS + OVER) // RING) * RING
SLOTS = JOBS * CAP


def multiplicity(delta):
    return ((delta >= 0) & (delta <= 128)).astype(np.float64) \
        + ((delta >= 0) & (delta % 4 == 0) & (delta <= 512)) + ((delta >= 0) & (delta % 16 == 0) & (delta <= 2048))


def slopes():
    def geometric(n):
        start = 2.0 ** (-8.0 / n)
        return [start ** (i + 1) for i in range(n)]
    return np.asarray(geometric(8) + geometric(16)[0::2][:HEADS - 8], np.float64)


def constants():
    f = np.float32
    p = np.arange(P)[:, None]
    delta = p + (SEQ - P) - np.arange(SEQ)[None, :]
    c = multiplicity(delta)
    lnc = np.where(c > 0, np.log(np.maximum(c, 1)), MASKED)
    sl = slopes()
    row = np.arange(HEADS * TDEC)
    head, q = row // TDEC, row % TDEC
    x = np.arange(PAST + TDEC)
    key = np.where(x < PAST, 4 * (x % P) + x // P, x)
    d2 = PAST + q[:, None] - key[None, :]
    c2 = multiplicity(d2)
    sbias = np.where(c2 > 0, np.log(np.maximum(c2, 1)) - sl[head][:, None] * d2, MASKED)
    window = np.asarray(WINDOWS)[(np.arange(POOLW) // 64)].reshape(2, P).T
    cnt = np.minimum(np.arange(16)[None, None, :] + 1, window[:, :, None])
    e = np.arange(EXPERTS)
    small = np.concatenate([
        np.tile(-sl, (P, 1)),
        1.0 / window,
        (1.0 / cnt).reshape(P, 32),
        np.tile(np.arange(8), (P, 1)),
        np.tile(e, (P, 1)),
        (np.arange(NT)[None, :] * P + p < TOK).astype(f),
        np.tile(np.arange(1, 12) * CAP, (P, 1)),
        np.tile(np.arange(JOBS) - EXPERTS, (P, 1)),
    ], axis=1)
    before = (e[None, :] < e[:, None]).astype(f).reshape(1, -1)
    return {
        "c_ident": np.eye(P, dtype=f),
        "c_tri": (p < np.arange(P)[None, :]).astype(f),
        "c_dist": np.maximum(delta, 0).astype(f),
        "c_lnc": lnc.astype(f),
        "c_sbias": sbias.astype(f),
        "c_small": small.astype(f),
        "c_before": np.tile(before, (P, 1)).astype(f),
        "c_tokid": (np.arange(NT)[None, :] * P + p).astype(np.int32),
    }


C_SLOPE, C_INVW, C_INVC, C_IOTA, C_EXP, C_VALID, C_STEP, C_JOB = 0, 12, 14, 46, 54, 86, 95, 106
C_SMALL = C_JOB + JOBS


def build(nc, d):
    hid = nc.dram_tensor("scratch_cat", (D, SEQ), F32, kind="Internal").ap()
    xfd = nc.dram_tensor("scratch_xf", (TOK, D), F32, kind="Internal").ap()
    lst = nc.dram_tensor("scratch_list", (SLOTS, 1), I32, kind="Internal").ap()
    yb = nc.dram_tensor("scratch_y", (SLOTS, D), F32, kind="Internal").ap()
    with ExitStack() as whole:
        ident = whole.enter_context(nc.sbuf_tensor("ident", [P, P], F32))
        small = whole.enter_context(nc.sbuf_tensor("small", [P, C_SMALL], F32))
        eps = whole.enter_context(nc.sbuf_tensor("eps", [P, 1], F32))
        turn = whole.enter_context(nc.semaphore("turn"))
        ut = whole.enter_context(nc.sbuf_tensor("ut", [P, 2, TOK], F32))
        qts = whole.enter_context(nc.sbuf_tensor("qts", [P, PAIRS, SMP], F32))
        cats = whole.enter_context(nc.sbuf_tensor("cats", [P, KD, SMP], F32))
        with ExitStack() as mixer:
            xh = mixer.enter_context(nc.sbuf_tensor("xh", [P, KD, TOK], F32R))
            xl = mixer.enter_context(nc.sbuf_tensor("xl", [P, KD, TOK], F32R))
            wraw = [mixer.enter_context(nc.sbuf_tensor(f"wraw{c}", [P, KD, P], F32)) for c in range(3)]
            wh = [mixer.enter_context(nc.sbuf_tensor(f"wh{c}", [P, KD, P], F32R)) for c in range(3)]
            wl = [mixer.enter_context(nc.sbuf_tensor(f"wl{c}", [P, KD, P], F32R)) for c in range(3)]
            norm_in(nc, d, ident, small, eps, xh, xl, wraw, wh, wl, lst)
            attention(nc, d, ident, small, turn, xh, xl, wraw, wh, wl, ut, qts, hid, yb)
        decode(nc, d, ident, small, ut, qts, cats, hid)
        with ExitStack() as moe:
            sb, _, sem = tools(nc, moe)
            lg = sb("lg", [P, NT, GROUPS + EXPERTS])
            gates, slot = sb("gates", [P, 2, NT]), sb("slot", [P, 2, NT], I32)
            jobs = sb("jobs", [P, JOBS + 1], I32)
            h = sb("h", [P, NT, D])
            project_out(nc, d, ident, eps, turn, cats, hid, xfd, h, lg)
            with ExitStack() as ring:
                sb, _, sem = tools(nc, ring)
                ins = Inputs()
                ins.wg, ins.wu = ([sb(f"f_{n}{r}", [P, KD, FF]) for r in range(RING)] for n in ("wg", "wu"))
                ins.wd = [sb(f"f_wd{r}", [P, 2, D]) for r in range(RING)]
                ins.idx = [sb(f"f_idx{r}", [CAP, 1], I32) for r in range(RING)]
                ins.xg = [sb(f"f_xg{r}", [CAP, D]) for r in range(RING)]
                ins.w_loaded, ins.wd_loaded, ins.idx_loaded, ins.gathered = (
                    [sem(f"f_{n}{r}") for r in range(RING)] for n in ("w_loaded", "wd_loaded", "idx_loaded", "gathered"))
                route(nc, d, small, turn, lg, gates, slot, jobs, lst, xfd, ins)
                experts(nc, d, ident, turn, jobs, lst, xfd, yb, ins)
            combine(nc, d, eps, h, gates, slot, yb)


class Inputs:
    pass


def load_gate_up(eng, d, ins, e, r):
    one = slice(e, e + 1) if isinstance(e, int) else bass.ds(e, 1)
    for dst, name in ((ins.wg, "w_gate"), (ins.wu, "w_up")):
        src = d[name].rearrange("l g e (p k) f -> (l g e) p (k f)", k=KD)
        eng.dma_start(dst[r][:].rearrange("p k f -> p (k f)"), src[one].rearrange("a p f -> p (a f)")).then_inc(ins.w_loaded[r], 16)


def load_down(eng, d, ins, e, r):
    one = slice(e, e + 1) if isinstance(e, int) else bass.ds(e, 1)
    src = d["w_down"].rearrange("l g e (p c) n -> (l g e) p (c n)", c=2)
    eng.dma_start(ins.wd[r][:].rearrange("p c n -> p (c n)"), src[one].rearrange("a p f -> p (a f)")).then_inc(ins.wd_loaded[r], 16)


def load_list(pool, ins, lst, j, r):
    lo = j * CAP
    at = slice(lo, lo + CAP) if isinstance(lo, int) else bass.ds(lo, CAP)
    pool.dma_start(ins.idx[r][:], lst[at, :]).then_inc(ins.idx_loaded[r], 16)


def gather_tokens(pool, ins, xfd, turn, i, r):
    pool.wait_ge(ins.idx_loaded[r], i * 16 + 16)
    pool.sem_inc(turn, 1)
    pool.indirect_dma_start(out=ins.xg[r][:], out_offset=None, in_=xfd,
                            in_offset=bass.IndirectOffsetOnAxis(ap=ins.idx[r][:].bitcast(U32), axis=0)).then_inc(ins.gathered[r], 16)


def tools(nc, ctx):
    return (lambda n, s, t=F32: ctx.enter_context(nc.sbuf_tensor(n, s, t)),
            lambda n, s, t=F32: ctx.enter_context(nc.psum_tensor(n, s, t)),
            lambda n: ctx.enter_context(nc.semaphore(n)))


def two_stages(eng, first, second):
    first(0, 0, 0, P)
    first(1, 0, 1, P)
    second(0, 0, 0, P)
    first(2, 1, 0, P)
    second(1, 0, 1, P)
    with eng.Fori(1, QT // 2 - 1) as i:
        first(i * 2 + 1, i, 1, P)
        second(i * 2, i, 0, P)
        first(i * 2 + 2, i + 1, 0, P)
        second(i * 2 + 1, i, 1, P)
    first(QT - 1, QT // 2 - 1, 1, P)
    second(QT - 2, QT // 2 - 1, 0, P)
    first(QT, QT // 2, 0, SMP)
    second(QT - 1, QT // 2 - 1, 1, P)
    second(QT, QT // 2, 0, SMP)


def later(i):
    return not isinstance(i, int) or i > 0


def norm_in(nc, d, ident, small, eps, xh, xl, wraw, wh, wl, lst):
    with ExitStack() as ctx:
        sb, ps, sem = tools(nc, ctx)
        xin = [sb(f"a_x{b}", [P, D]) for b in range(2)]
        xn = [sb(f"a_xn{b}", [P, D]) for b in range(2)]
        junk = sb("a_junk", [P, D])
        gm = sb("a_g", [P, D])
        ssq = [sb(f"a_ssq{b}", [P, 1]) for b in range(2)]
        std = [sb(f"a_std{b}", [P, 1]) for b in range(2)]
        rin = [sb(f"a_rin{b}", [P, 1]) for b in range(2)]
        zero = sb("a_zero", [P, SLOTS // P], I32)
        xt = [ps(f"a_xt{b}", [P, KD, P]) for b in range(2)]
        g_loaded, ident_loaded, x_loaded = sem("a_g_loaded"), sem("a_ident_loaded"), [sem(f"a_loaded{b}") for b in range(2)]
        squared, rooted, inverted, normed = sem("a_squared"), sem("a_rooted"), sem("a_inverted"), sem("a_normed")
        turned, hi_done, lo_done, zeroed, listed = sem("a_turned"), sem("a_hi"), sem("a_lo"), sem("a_zeroed"), sem("a_listed")
        eps_set, w_loaded, w_hi = sem("a_eps_set"), sem("a_w_loaded"), sem("a_w_hi")
        xp = d["x_prompt"].rearrange("a t d -> (a t) d")
        xs = d["x_sample"].rearrange("a t d -> (a t) d")
        w_in = d["w_in"].rearrange("l (k p) c -> p (l k) c", p=P)
        block = ctx.enter_context(nc.Block())

        @block.sync
        def _(sp):
            def load(t, i, b, src, n):
                if later(i):
                    sp.wait_ge(normed, t - 1)
                sp.dma_start(xin[b][:n, :], src).then_inc(x_loaded[b], 16)
            load(0, 0, 0, xp[0:P, :], P)
            load(1, 0, 1, xp[P:2 * P, :], P)
            with sp.Fori(1, QT // 2) as i:
                for b in range(2):
                    load(i * 2 + b, i, b, xp[bass.ds(i * (2 * P) + b * P, P), :], P)
            load(QT, QT // 2, 0, xs, SMP)
            sp.wait_ge(zeroed, 1)
            sp.dma_start(lst.rearrange("(p a) b -> p (a b)", p=P), zero[:]).then_inc(listed, 16)
            sp.wait_ge(listed, 16)

        @block.gpsimd
        def _(pool):
            pool.dma_start(gm[:], d["g_mix"].partition_broadcast(P).rearrange("p a d -> p (a d)")).then_inc(g_loaded, 16)
            pool.dma_start(ident[:], d["c_ident"]).then_inc(ident_loaded, 16)
            pool.dma_start(small[:], d["c_small"]).then_inc(ident_loaded, 16)
            for c in range(3):
                pool.dma_start(wraw[c][:], w_in[:, :, POOLW + c * ATTW:POOLW + c * ATTW + P]).then_inc(w_loaded, 16)
            pool.wait_ge(w_loaded, 48)
            for c in range(3):
                nc.gpsimd.tensor_copy(wh[c][:], wraw[c][:]).then_inc(w_hi, 1)
                pool.wait_ge(w_hi, c + 1)
                nc.gpsimd.tensor_tensor(wl[c][:], wraw[c][:], wh[c][:].bitcast(F32), ALU.subtract)

        @block.scalar
        def _(act):
            def norm(t, i, b, n):
                act.wait_ge(x_loaded[b], (i + 1) * 16)
                nc.scalar.activation(junk[:n, :], xin[b][:n, :], ACT.Square, accum_out=ssq[b][:n, :]).then_inc(squared, 1)
                act.wait_ge(squared, t + 1)
                nc.scalar.activation(std[b][:n, :], ssq[b][:n, :], ACT.Sqrt, bias=eps[:n, :], scale=1.0 / D).then_inc(rooted, 1)

            def split(t, i, b, n):
                act.wait_ge(turned, t + 1)
                nc.scalar.activation(xh[:, :, token(t, n)], xt[b][:, :, :n], ACT.Copy).then_inc(hi_done, 1)
            act.wait_ge(eps_set, 1)
            two_stages(act, norm, split)

        @block.vector
        def _(dve):
            nc.vector.memset(eps[:], EPS).then_inc(eps_set, 1)
            nc.vector.memset(zero[:], 0).then_inc(zeroed, 1)
            dve.wait_ge(g_loaded, 16)

            def norm(t, i, b, n):
                dve.wait_ge(rooted, t + 1)
                nc.vector.reciprocal(rin[b][:n, :], std[b][:n, :]).then_inc(inverted, 1)
                dve.wait_ge(inverted, t + 1)
                nc.vector.scalar_tensor_tensor(xn[b][:n, :], xin[b][:n, :], rin[b][:n, :], gm[:n, :],
                                               ALU.mult, ALU.mult).then_inc(normed, 1)

            def split(t, i, b, n):
                dve.wait_ge(hi_done, t + 1)
                nc.vector.tensor_tensor(xl[:, :, token(t, n)], xt[b][:, :, :n],
                                        xh[:, :, token(t, n)].bitcast(F32), ALU.subtract).then_inc(lo_done, 1)
            two_stages(dve, norm, split)

        @block.tensor
        def _(pe):
            pe.wait_ge(ident_loaded, 32)

            def turned_tile(t, b, n):
                pe.wait_ge(normed, t + 1)
                if not isinstance(t, int) or t >= 2:
                    pe.wait_ge(lo_done, t - 1)
                for k in range(KD):
                    last = nc.tensor.transpose(xt[b][:, k, :n], xn[b][:n, k * P:(k + 1) * P], ident[:n, :n])
                last.then_inc(turned, 1)
            for b in range(2):
                turned_tile(b, b, P)
            with pe.Fori(1, QT // 2) as i:
                for b in range(2):
                    turned_tile(i * 2 + b, b, P)
            turned_tile(QT, 0, SMP)


def token(t, n):
    return slice(t * P, t * P + n) if isinstance(t, int) else bass.ds(t * P, n)


TB = [(0, 364), (364, 364), (728, TOK - 728)]
UNIT_STEPS = [[0, 1], [2], [3, 4], [5, 6], [7], [8, 9], [10, 11], [12], [13, 14]]
STEPS = [(a, i) for a in range(2) for i in range(QT)]
NAT = [("k", (0, 4)), ("k", (4, 7)), ("k", (7, 9)), ("v", (0, 4)), ("v", (4, 7)), ("v", (7, 9))]
FILLS = [("nat", x) for x in NAT] + [("p", (s, c)) for s, (a, i) in enumerate(STEPS) for c in range(-(-(i + 1) // 4))] \
    + [("o", 0), ("o", 1)]
NF = len(FILLS) // 2
assert len(FILLS) % 2 == 0
S = len(STEPS)
U = len(UNIT_STEPS)


def attention(nc, d, ident, small, turn, xh, xl, wraw, wh, wl, ut, qts, hid, yb):
    with ExitStack() as ctx:
        sb, ps, sem = tools(nc, ctx)
        raw = [sb(f"b_raw{n}", [P, SEQ if n == "q" else TOK]) for n in "qkv"]
        qs = [sb(f"b_qs{a}", [P, SEQ], F32R) for a in range(2)]
        kh = [sb(f"b_kh{a}", [P, SEQ], F32R) for a in range(2)]
        kl = [sb(f"b_kl{a}", [P, SEQ], F32R) for a in range(2)]
        bias = [sb(f"b_bias{a}", [P, SEQ]) for a in range(2)]
        dist, lnc = sb("b_dist", [P, SEQ]), sb("b_lnc", [P, SEQ])
        nslope = [sb(f"b_nslope{a}", [P, 1]) for a in range(2)]
        nat = {n: sb(f"b_nat{n}", [P, NT, P]) for n in "kv"}
        sc = [sb(f"b_s{b}", [P, SEQ]) for b in range(2)]
        pt = [sb(f"b_pt{b}", [P, SEQ]) for b in range(2)]
        zero = sb("b_zero", [P, 256])
        onat = sb("b_onat", [P, QT, P])
        otr = sb("b_otr", [P, SEQ])
        nmax, den, inv = sb("b_nmax", [P, 4]), sb("b_den", [P, 4]), sb("b_inv", [P, 4])
        scp = [ps(f"b_scp{b}", [P, SEQ]) for b in range(2)]
        tp = [ps(f"b_tp{b}", [P, 512]) for b in range(2)]
        pj, op = ps("b_pj", [P, 512]), ps("b_op", [P, 512])

        consts = sem("b_consts")
        wraw_loaded = [sem(f"b_wraw_loaded{c}") for c in range(3)]
        w_hi, w_lo = sem("b_w_hi"), sem("b_w_lo")
        proj_done, proj_evac = sem("b_proj_done"), sem("b_proj_evac")
        stk_act = [sem(f"b_stk_act{a}") for a in range(2)]
        stk_dve = [sem(f"b_stk_dve{a}") for a in range(2)]
        stk_pool = [sem(f"b_stk_pool{a}") for a in range(2)]
        slope_cur = sem("b_slope")
        scores_ready, smax_done, exp_done = sem("b_scores"), sem("b_smax"), sem("b_exp")
        filled = [sem(f"b_filled{b}") for b in range(2)]
        evac = [sem(f"b_evac{b}") for b in range(2)]
        pv_done, inverted, o_evac = sem("b_pv"), sem("b_inverted"), sem("b_o_evac")
        kv_out, ot_out, pool_out = sem("b_kv_out"), sem("b_ot_out"), sem("b_pool_out")
        zeroed, y_cleared = sem("b_zeroed"), sem("b_y_cleared")
        block = ctx.enter_context(nc.Block())

        w_in = d["w_in"].rearrange("l (k p) c -> p (l k) c", p=P)
        hidv = hid
        kp, vp = (d[n].rearrange("l b (t p) h e -> p (l b t) (h e)", p=P) for n in ("o_k_prompt", "o_v_prompt"))
        ksm, vsm = (d[n].rearrange("l b t h e -> (l b t) (h e)") for n in ("o_k_sample", "o_v_sample"))

        def chunks(nk):
            return [(c, min(4, nk - 4 * c)) for c in range(-(-nk // 4))]

        def fill_of(kind, key):
            n = FILLS.index((kind, key))
            return n % 2, n // 2

        @block.sync
        def _(sp):
            sp.dma_start(dist[:], d["c_dist"]).then_inc(consts, 16)
            sp.dma_start(lnc[:], d["c_lnc"]).then_inc(consts, 16)

            def load_w(j, c, col):
                sp.wait_ge(w_lo, j * 3 + c + 1)
                sp.dma_start(wraw[c][:], w_in[:, :, col]).then_inc(wraw_loaded[c], 16)

            def store(p):
                for n, (b, m) in (("k", fill_of(*FILLS[2])), ("v", fill_of(*FILLS[5]))):
                    for bb in range(2):
                        last = max(k // 2 for k in range(6) if k % 2 == bb and NAT[k][0] == n)
                        sp.wait_ge(evac[bb], p * NF + last + 2)
                        sp.sem_inc(turn, 1)
                    big, sml = (kp, ksm) if n == "k" else (vp, vsm)
                    sp.dma_start(big[:, :, cols(p)], nat[n][:, 0:QT, :]).then_inc(kv_out, 16)
                    sp.dma_start(sml[:, cols(p)], nat[n][0:SMP, QT, :]).then_inc(kv_out, 16)
                for bb in range(2):
                    sp.wait_ge(evac[bb], (p + 1) * NF + 1)
                    sp.sem_inc(turn, 1)
                sp.dma_start(hidv[rows(p), :], otr[:]).then_inc(ot_out, 16)

            def cols(p):
                return slice(p * P, p * P + P) if isinstance(p, int) else bass.ds(p * P, P)

            def rows(p):
                return slice(POOLW + p * P, POOLW + p * P + P) if isinstance(p, int) else bass.ds(p * P + POOLW, P)

            def wcol(j, c):
                base = POOLW + c * ATTW
                return slice(base + j * P, base + j * P + P) if isinstance(j, int) else bass.ds(j * P + base, P)

            for c in range(3):
                load_w(1, c, wcol(1, c))
            sp.wait_ge(zeroed, 1)
            spare = yb[EXPERTS * CAP:SLOTS, :].rearrange("(p a) (c n) -> p (a c) n", p=P, n=256)
            sp.dma_start(spare, zero[:].unsqueeze(1).to_broadcast([P, spare.shape[1], 256])).then_inc(y_cleared, 16)
            with sp.Fori(0, PAIRS - 2) as p:
                for c in range(3):
                    load_w(p + 2, c, wcol(p + 2, c))
                store(p)
            for c in range(2):
                load_w(PAIRS, c, slice(c * P, c * P + P))
            for p in range(PAIRS - 2, PAIRS):
                store(p)
            sp.wait_ge(y_cleared, 16)
            sp.wait_ge(kv_out, PAIRS * 64 + 1)
            sp.wait_ge(ot_out, PAIRS * 16 + 1)

        @block.gpsimd
        def _(pool):
            pool.sem_inc(w_lo, 6)
            nc.gpsimd.memset(zero[:], 0.0).then_inc(zeroed, 1)
            pool.wait_ge(zeroed, 1)
            pool.wait_ge(consts, 32)

            def split_w(j, c):
                pool.wait_ge(wraw_loaded[c], j * 16)
                pool.wait_ge(proj_done, (j - 1) * U + 3 * c + 3)
                pool.sem_inc(turn, 1)
                nc.gpsimd.tensor_copy(wh[c][:], wraw[c][:]).then_inc(w_hi, 1)
                pool.wait_ge(w_hi, j * 3 + c - 2)
                nc.gpsimd.tensor_tensor(wl[c][:], wraw[c][:], wh[c][:].bitcast(F32), ALU.subtract).then_inc(w_lo, 1)

            def head_part(a, p, before, first=False):
                pool.wait_ge(*before)
                pool.wait_ge(stk_act[a], p * 3 + 2)
                nc.gpsimd.tensor_tensor(kl[a][r64(a), :], raw[1][r64(a), 0:SEQ], kh[a][r64(a), :].bitcast(F32),
                                        ALU.subtract).then_inc(stk_pool[a], 1)
                pool.wait_ge(stk_pool[a], p * 3 + 1)
                nc.gpsimd.tensor_tensor(kl[a][r64(1 - a), :], raw[1][r64(a), 0:SEQ], kh[a][r64(a), :].bitcast(F32),
                                        ALU.subtract).then_inc(stk_pool[a], 1)
                pool.wait_ge(stk_pool[a], p * 3 + 2)
                pool.sem_inc(turn, 1)
                nc.gpsimd.tensor_copy(nslope[a][:], small[:, col1(p, a)]).then_inc(slope_cur, 1)
                pool.wait_ge(slope_cur, p * 4 + 2 * a + 1)
                if not first:
                    pool.wait_ge(smax_done, p * S - S + 8 * a + 8 + 2)
                pool.sem_inc(turn, 1)
                nc.gpsimd.tensor_scalar(bias[a][:], dist[:], nslope[a][:], None, ALU.mult).then_inc(slope_cur, 1)
                pool.wait_ge(slope_cur, p * 4 + 2 * a + 2)
                nc.gpsimd.tensor_tensor(bias[a][:], bias[a][:], lnc[:], ALU.add).then_inc(stk_pool[a], 1)

            def col1(p, a):
                return slice(2 * p + a, 2 * p + a + 1) if isinstance(p, int) else bass.ds(p * 2 + a, 1)

            head_part(0, 0, (w_lo, 3 + 3), first=True)
            for c in range(3):
                split_w(1, c)
            head_part(1, 0, (w_lo, 6 + 3), first=True)

            def body(p, more):
                split_w(p + 2, 0)
                split_w(p + 2, 1)
                head_part(0, p + 1, (w_lo, p * 3 + 6 + 2 + 3))
                if more:
                    split_w(p + 2, 2)
                    head_part(1, p + 1, (w_lo, p * 3 + 9 + 3))
                else:
                    head_part(1, p + 1, (stk_pool[0], p * 3 + 6))
            with pool.Fori(0, PAIRS - 2) as p:
                body(p, True)
            body(PAIRS - 2, False)

        def split_act(act, a, p, part):
            if part == 0:
                nc.scalar.activation(qs[a][r64(a), :], raw[0][r64(a), :], ACT.Copy).then_inc(stk_act[a], 1)
            elif part == 1:
                nc.scalar.activation(kh[a][r64(a), :], raw[1][r64(a), 0:SEQ], ACT.Copy).then_inc(stk_act[a], 1)
            else:
                nc.scalar.activation(kh[a][r64(1 - a), :], raw[1][r64(a), 0:SEQ], ACT.Copy).then_inc(stk_act[a], 1)

        def evac_fill(eng, copy, p, n):
            kind, key = FILLS[n]
            b, m = n % 2, n // 2
            eng.wait_ge(filled[b], p * NF + m + 1)
            if kind == "nat":
                name, (t0, t1) = key
                full = min(t1, QT) - t0
                if t1 > QT:
                    copy(nat[name][:SMP, QT, :], tp[b][:SMP, full * P:(full + 1) * P])
                copy(nat[name][:, t0:t0 + full, :], tp[b][:, 0:full * P].rearrange("p (t c) -> p t c", c=P)).then_inc(evac[b], 1)
            elif kind == "p":
                s, c = key
                w = dict(chunks(STEPS[s][1] + 1))[c] * P
                copy(pt[s % 2][:, 512 * c:512 * c + w], tp[b][:, 0:w]).then_inc(evac[b], 1)
            else:
                copy(otr[:, 512 * key:512 * key + 512], tp[b][:, :]).then_inc(evac[b], 1)

        def step_fills(s, b):
            return [n for n, (kind, key) in enumerate(FILLS) if kind == "p" and key[0] == s and n % 2 == b]

        @block.scalar
        def _(act):
            act.sem_inc(evac[0], 1)
            copy = lambda o, i: nc.scalar.activation(o, i, ACT.Copy)

            def exp(p, s):
                a, i = STEPS[s]
                w = (i + 1) * P
                act.wait_ge(smax_done, p * S + s + 3)
                nc.scalar.activation(sc[s % 2][:, 0:w], sc[s % 2][:, 0:w], ACT.Exp, bias=nmax[:, s % 4:s % 4 + 1],
                                     scale=-1.0, accum_out=den[:, s % 4:s % 4 + 1]).then_inc(exp_done, 1)

            def split_a(p, part):
                if part == 0:
                    act.wait_ge(proj_evac, p * U + 6)
                    if not isinstance(p, int) or p > 0:
                        act.wait_ge(scores_ready, p * S - S + 8 + 1)
                split_act(act, 0, p, part)

            def body(p, last):
                act.wait_ge(kv_out, p * 64 + 1)
                act.wait_ge(pv_done, p * S + 2)
                for n in (0, 2, 4):
                    evac_fill(act, copy, p, n)
                act.wait_ge(scores_ready, p * S + 1)
                split_act(act, 1, p, 0)
                exp(p, 0)
                for s in range(S):
                    act.wait_ge(pv_done, p * S + s + 1)
                    for n in step_fills(s, 0):
                        evac_fill(act, copy, p, n)
                    if s + 1 < S:
                        exp(p, s + 1)
                    if s < 2:
                        split_act(act, 1, p, s + 1)
                    if not last and 10 <= s < 13:
                        split_a(p + 1, s - 10)
                act.wait_ge(ot_out, p * 16 + 1)
                evac_fill(act, copy, p, len(FILLS) - 2)
            for part in range(3):
                split_a(0, part)
            with act.Fori(0, PAIRS - 1) as p:
                body(p, False)
            body(PAIRS - 1, True)

        @block.vector
        def _(dve):
            dve.sem_inc(evac[1], 1)
            dve.sem_inc(smax_done, 2)
            dve.sem_inc(o_evac, 1)
            dve.sem_inc(kv_out, 1)
            dve.sem_inc(ot_out, 1)
            copy = nc.vector.tensor_copy

            def wait_scores(p, s):
                if s in (0, 8):
                    dve.wait_ge(stk_pool[STEPS[s][0]], p * 3 + 3)
                dve.wait_ge(scores_ready, p * S + s + 2)

            def out_evac(p, s):
                a, i = STEPS[s]
                nc.vector.tensor_scalar(onat[:, i, 64 * a:64 * a + 64], op[:, 0:HD], inv[:, s % 4:s % 4 + 1], None,
                                        ALU.mult).then_inc(o_evac, 1)

            def smax(p, s):
                a, i = STEPS[s]
                w = (i + 1) * P
                nc.vector.tensor_tensor_reduce(
                    out=sc[s % 2][:, 0:w], in0=scp[s % 2][:, 0:w], in1=bias[a][:, SEQ - w:SEQ], scale=-1.0, scalar=BIG,
                    op0=ALU.add, op1=ALU.min, accum_out=nmax[:, s % 4:s % 4 + 1]).then_inc(smax_done, 1)

            def evac_proj(p, u, kind="qkv"):
                c, (t0, n) = u // 3, TB[u % 3]
                dve.wait_ge(proj_done, p * U + u + 1)
                if kind == "u":
                    nc.vector.tensor_copy(ut[:, c, t0:t0 + n], pj[:, 0:n]).then_inc(proj_evac, 1)
                elif c == 0 and u == 2:
                    col = slice(p, p + 1) if isinstance(p, int) else bass.ds(p, 1)
                    nc.vector.tensor_scalar(qts[:, col, :].rearrange("p a t -> p (a t)"), pj[:, SEQ - t0:n], SCALE, None, ALU.mult)
                    nc.vector.tensor_scalar(raw[0][:, t0:SEQ], pj[:, 0:SEQ - t0], SCALE, None, ALU.mult).then_inc(proj_evac, 1)
                elif c == 0:
                    nc.vector.tensor_scalar(raw[0][:, t0:t0 + n], pj[:, 0:n], SCALE, None, ALU.mult).then_inc(proj_evac, 1)
                else:
                    if u == 3 and (not isinstance(p, int) or p > 0):
                        dve.wait_ge(stk_pool[1], p * 3 - 1)
                        dve.wait_ge(stk_act[1], p * 3)
                    nc.vector.tensor_copy(raw[c][:, t0:t0 + n], pj[:, 0:n]).then_inc(proj_evac, 1)

            def q_lo(a, p):
                dve.wait_ge(stk_act[a], p * 3 + 1)
                nc.vector.tensor_tensor(qs[a][r64(1 - a), :], raw[0][r64(a), :], qs[a][r64(a), :].bitcast(F32),
                                        ALU.subtract).then_inc(stk_dve[a], 1)

            def body(p, last):
                dve.wait_ge(kv_out, p * 64 + 1)
                for n in (1, 3):
                    evac_fill(dve, copy, p, n)
                wait_scores(p, 0)
                dve.wait_ge(scores_ready, p * S + 3)
                evac_fill(dve, copy, p, 5)
                smax(p, 0)
                for s in range(S):
                    a, i = STEPS[s]
                    if s + 1 < S:
                        if s >= 1:
                            dve.wait_ge(inverted, p * S + s)
                            wait_scores(p, s + 1)
                            out_evac(p, s - 1)
                        smax(p, s + 1)
                    for n in step_fills(s, 1):
                        evac_fill(dve, copy, p, n)
                    for u in range(6 if last else U):
                        if UNIT_STEPS[u][-1] == s:
                            evac_proj(p + 1, u, "u" if last else "qkv")
                    if s == 0:
                        q_lo(1, p)
                    dve.wait_ge(exp_done, p * S + s + 1)
                    nc.vector.reciprocal(inv[:, s % 4:s % 4 + 1], den[:, s % 4:s % 4 + 1]).then_inc(inverted, 1)
                    if s >= S - 2:
                        dve.wait_ge(inverted, p * S + s + 1)
                        dve.wait_ge(pv_done, p * S + s + 3)
                        out_evac(p, s)
                    if not last and s == 12:
                        q_lo(0, p + 1)
                dve.wait_ge(ot_out, p * 16 + 1)
                evac_fill(dve, copy, p, len(FILLS) - 1)
            for u in range(U):
                evac_proj(0, u)
            q_lo(0, 0)
            with dve.Fori(0, PAIRS - 1) as p:
                body(p, False)
            body(PAIRS - 1, True)

        @block.tensor
        def _(pe):
            pe.sem_inc(scores_ready, 1)
            pe.sem_inc(pv_done, 2)

            def project(j, u, part, parts):
                c, (t0, n) = u // 3, TB[u % 3]
                order = [(k, w, x) for k in range(KD) for w, x in ((wh[c], xh), (wl[c], xh), (wh[c], xl))]
                if part == 0:
                    pe.wait_ge(w_lo, j * 3 + c + 1 + 3)
                    if u or not isinstance(j, int) or j > 0:
                        pe.wait_ge(proj_evac, j * U + u)
                lo, hi = len(order) * part // parts, len(order) * (part + 1) // parts
                for q in range(lo, hi):
                    k, w, x = order[q]
                    last = nc.tensor.matmul(pj[:, 0:n], w[:, k, :], x[:, k, t0:t0 + n],
                                            start=(q == 0), stop=(q == len(order) - 1))
                if part == parts - 1:
                    last.then_inc(proj_done, 1)

            def take_bank(p, n):
                pe.wait_ge(evac[n % 2], p * NF + n // 2 + 1)

            def scores(p, s):
                a, i = STEPS[s]
                if s in (0, 8):
                    pe.wait_ge(stk_act[a], p * 3 + 3)
                    pe.wait_ge(stk_dve[a], p + 1)
                    pe.wait_ge(stk_pool[a], p * 3 + 2)
                pe.wait_ge(smax_done, p * S + s + 1)
                for c, m in chunks(i + 1):
                    o = scp[s % 2][:, 512 * c:512 * c + m * P]
                    q = qs[a][:, i * P:(i + 1) * P]
                    nc.tensor.matmul(o, q, kh[a][:, 512 * c:512 * c + m * P], start=True, stop=False)
                    last = nc.tensor.matmul(o, q, kl[a][:, 512 * c:512 * c + m * P], start=False, stop=True)
                last.then_inc(scores_ready, 1)

            def body(p, last_pair):
                pe.wait_ge(proj_evac, p * U + U)
                for n in range(6):
                    name, (t0, t1) = NAT[n]
                    take_bank(p, n)
                    for t in range(t0, t1):
                        w = SMP if t == QT else P
                        last = nc.tensor.transpose(tp[n % 2][:w, (t - t0) * P:(t - t0 + 1) * P],
                                                   raw[1 if name == "k" else 2][:, t * P:t * P + w], ident[:])
                    last.then_inc(filled[n % 2], 1)
                    if n in (1, 3):
                        scores(p, n // 2)
                for s in range(S):
                    a, i = STEPS[s]
                    if 0 < s < S - 1:
                        scores(p, s + 1)
                    pe.wait_ge(exp_done, p * S + s + 1)
                    for c, m in chunks(i + 1):
                        n = FILLS.index(("p", (s, c)))
                        take_bank(p, n)
                        for j in range(m):
                            last = nc.tensor.transpose(tp[n % 2][:, j * P:(j + 1) * P],
                                                       sc[s % 2][:, (4 * c + j) * P:(4 * c + j + 1) * P], ident[:])
                        last.then_inc(filled[n % 2], 1)
                    for u in range(6 if last_pair else U):
                        for part, st in enumerate(UNIT_STEPS[u]):
                            if st == s:
                                project(p + 1, u, part, len(UNIT_STEPS[u]))
                    for b in range(2):
                        mine = step_fills(s, b)
                        if mine:
                            pe.wait_ge(evac[b], p * NF + mine[-1] // 2 + 2)
                    if s == 0:
                        for b in range(2):
                            pe.wait_ge(evac[b], p * NF + 3 + 1)
                    pe.wait_ge(o_evac, p * S + s + 1)
                    for j in range(i + 1):
                        last = nc.tensor.matmul(op[:, 0:HD], pt[s % 2][:, j * P:(j + 1) * P],
                                                nat["v"][:, j, HD * a:HD * a + HD], start=(j == 0), stop=(j == i))
                    last.then_inc(pv_done, 1)
                pe.wait_ge(o_evac, p * S + S + 1)
                for n in (len(FILLS) - 2, len(FILLS) - 1):
                    take_bank(p, n)
                    for j in range(4):
                        t = 4 * FILLS[n][1] + j
                        last = nc.tensor.transpose(tp[n % 2][:, j * P:(j + 1) * P], onat[:, t, :], ident[:])
                    last.then_inc(filled[n % 2], 1)
            for u in range(U):
                project(0, u, 0, 1)
            with pe.Fori(0, PAIRS - 1) as p:
                body(p, False)
            body(PAIRS - 1, True)


def r64(a):
    return slice(64 * a, 64 * a + 64)


KEYS = PAST + TDEC
SROWS = HEADS * TDEC
MIXES = [(0, 512), (512, 512), (SEQ, SMP)]


def decode(nc, d, ident, small, ut, qts, cats, hid):
    with ExitStack() as ctx:
        sb, ps, sem = tools(nc, ctx)
        kc = [sb(f"c_k{b}", [P, 4, ATTW]) for b in range(2)]
        vc = [sb(f"c_v{b}", [P, 4, ATTW]) for b in range(2)]
        kn = [sb(f"c_kn{b}", [TDEC, ATTW]) for b in range(2)]
        vn = [sb(f"c_vn{b}", [TDEC, ATTW]) for b in range(2)]
        kt = [sb(f"c_kt{b}", [P, PAIRS, KEYS]) for b in range(2)]
        qb = [sb(f"c_qb{b}", [P, PAIRS * 112]) for b in range(2)]
        sbias = sb("c_bias", [SROWS, KEYS])
        s_ = [sb(f"c_s{b}", [SROWS, KEYS]) for b in range(2)]
        pts = [sb(f"c_pt{b}", [P, 5 * SROWS]) for b in range(2)]
        nmax, den, inv = sb("c_nmax", [SROWS, 2]), sb("c_den", [SROWS, 2]), sb("c_inv", [SROWS, 2])
        spare = sb("c_spare", [SROWS, 1])
        ktp = [ps(f"c_ktp{b}", [P, 512]) for b in range(2)]
        on = sb("c_on", [SROWS, ATTW])
        scp = ps("c_scp", [P, 2 * 512])
        pvp = [ps(f"c_pvp{o}", [P, 512]) for o in range(2)]
        ptp, xp = ps("c_ptp", [P, 512]), ps("c_xp", [P, 512])
        picked = xp[:, P:P + PAIRS * 16]
        pe_ = sb("c_pe", [P, 2, 1, POOL_STATE + SEQ])
        se = sb("c_se", [P, 2, NSEQ, POOL_STATE + TDEC])
        pw = [sb(f"c_pw{n}", [P, 1, POOL_STATE + SEQ]) for n in range(2)]
        sw = [sb(f"c_sw{n}", [P, NSEQ, POOL_STATE + TDEC]) for n in range(2)]
        zt = sb("c_zt", [P, 2, TOK])
        wp = sb("c_wp", [P, 2, P])
        psc = sb("c_psc", [P, 2])
        pc = sb("c_pc", [P, 2, SEQ])
        stn = sb("c_stn", [NSEQ * POOL_STATE, POOLW])
        un = sb("c_un", [P, 2, 2, P])

        state_loaded, bias_loaded, mix_loaded = sem("c_state"), sem("c_bias_loaded"), sem("c_mix_loaded")
        k_loaded, v_loaded = ([sem(f"c_{n}_loaded{b}") for b in range(2)] for n in "kv")
        qb_ready = sem("c_qb_ready")
        kt_filled, kt_evac = [sem(f"c_kt_filled{b}") for b in range(2)], [sem(f"c_kt_evac{b}") for b in range(2)]
        kn_filled, kn_evac = sem("c_kn_filled"), sem("c_kn_evac")
        sc_done, sm_done, ex_done, inverted, pn_done = (sem("c_" + n) for n in ("scores", "smax", "exp", "inv", "norm"))
        pt_filled, pt_evac, pv_done, on_act, on_dve, sel_done, o_evac = (
            sem("c_" + n) for n in ("pt_filled", "pt_evac", "pv", "on_act", "on_dve", "sel_done", "o_evac"))
        st_filled, st_evac, un_filled, un_evac = (sem("c_" + n) for n in ("st_filled", "st_evac", "un_filled", "un_evac"))
        pooling, zeroed, z_ready, mixed, mix_evac = (sem("c_" + n) for n in ("pooling", "zeroed", "z_ready", "mixed", "mix_evac"))
        out = sem("c_out")
        block = ctx.enter_context(nc.Block())
        ck, cv = (d[n].rearrange("l s (p j) h e -> (l s) p j (h e)", j=4) for n in ("cache_k", "cache_v"))
        nk, nv = (d[n].rearrange("l s t h e -> (l s) t (h e)") for n in ("o_k_sample", "o_v_sample"))

        def order(eng, kq, pv, out, pick, mix):
            def step(s, i, b, s1, i1, b1):
                kq(s1, i1, b1, lambda: pv(s, i, b), lambda: out(s, i, b))
                pick(s, i, b)
            kq(0, 0, 0, None, None)
            step(0, 0, 0, 1, 0, 1)
            step(1, 0, 1, 2, 1, 0)
            with eng.Fori(1, NSEQ // 2 - 1) as i:
                step(i * 2, i, 0, i * 2 + 1, i, 1)
                step(i * 2 + 1, i, 1, i * 2 + 2, i + 1, 0)
            step(NSEQ - 2, NSEQ // 2 - 1, 0, NSEQ - 1, NSEQ // 2 - 1, 1)
            mix()
            pv(NSEQ - 1, NSEQ // 2 - 1, 1)
            out(NSEQ - 1, NSEQ // 2 - 1, 1)
            pick(NSEQ - 1, NSEQ // 2 - 1, 1)

        @block.sync
        def _(sp):
            def one(s):
                return slice(s, s + 1) if isinstance(s, int) else bass.ds(s, 1)

            def load_k(s, i, b):
                if later(i):
                    sp.wait_ge(sc_done, s - 1)
                sp.dma_start(kc[b][:], ck[one(s), :, :, :].rearrange("a p j c -> p (a j) c")).then_inc(k_loaded[b], 16)
                sp.dma_start(kn[b][:], nk[one(s), :, :].rearrange("a t c -> t (a c)")).then_inc(k_loaded[b], 16)

            def load_v(s, i, b):
                if later(i):
                    sp.wait_ge(pv_done, s - 1)
                sp.dma_start(vc[b][:], cv[one(s), :, :, :].rearrange("a p j c -> p (a j) c")).then_inc(v_loaded[b], 16)
                sp.dma_start(vn[b][:], nv[one(s), :, :].rearrange("a t c -> t (a c)")).then_inc(v_loaded[b], 16)
            sp.dma_start(stn[:], d["state_pool"].rearrange("l s t c -> (l s t) c")).then_inc(state_loaded, 16)
            load_k(0, 0, 0)
            sp.dma_start(sbias[:], d["c_sbias"]).then_inc(bias_loaded, 16)
            load_k(1, 0, 1)
            load_v(0, 0, 0)
            load_v(1, 0, 1)
            with sp.Fori(1, NSEQ // 2) as i:
                for b in range(2):
                    load_k(i * 2 + b, i, b)
                    load_v(i * 2 + b, i, b)
            pp, psm = d["o_pool_prompt"], d["o_pool_sample"]
            sp.wait_ge(un_evac, 2)
            sp.dma_start(pp.rearrange("l b t (c p) -> (l b t) c p", c=2), un[P - POOL_STATE:P, :, 0, :]).then_inc(out, 16)
            n_old = POOL_STATE - TDEC
            sp.dma_start(psm[0, :, 0:n_old, :], d["state_pool"][0, :, TDEC:POOL_STATE, :]).then_inc(out, 16)
            for s in range(NSEQ):
                sp.dma_start(psm[0, s, n_old:POOL_STATE, :].rearrange("t (c p) -> t c p", c=2),
                             un[s * TDEC:(s + 1) * TDEC, :, 1, :]).then_inc(out, 16)
            sp.wait_ge(mix_evac, 6)
            sp.dma_start(hid[0:POOLW, :].rearrange("(c p) t -> p c t", p=P), pc[:]).then_inc(out, 16)
            sp.wait_ge(out, (3 + NSEQ) * 16)

        @block.gpsimd
        def _(pool):
            nc.gpsimd.memset(wp[:], 0.0).then_inc(zeroed, 1)
            nc.gpsimd.memset(qb[0][:], 0.0).then_inc(zeroed, 1)
            nc.gpsimd.memset(qb[1][:], 0.0).then_inc(zeroed, 1)
            pool.wait_ge(zeroed, 3)
            pool.dma_start(psc[:], d["pool_scale"].rearrange("l (c p) -> p (l c)", p=P), allow_slow_non_contiguous=True).then_inc(mix_loaded, 16)
            for g in range(GROUPS):
                a = g % 2
                pool.dma_start(wp[r64(a), g // 2, r64(a)], d["w_pool"][0, g, :, :]).then_inc(mix_loaded, 16)
            n = [0]

            def link(ins):
                n[0] += 1
                ins.then_inc(pooling, 1)
                pool.wait_ge(pooling, n[0])
            link(nc.gpsimd.memset(pe_[:, :, :, 0:POOL_STATE], 0.0))
            link(nc.gpsimd.tensor_copy(pe_[:, :, 0, POOL_STATE:], ut[:, :, 0:SEQ]))
            for c in range(2):
                link(nc.gpsimd.tensor_copy(se[:, c, :, POOL_STATE:], ut[:, c, SEQ:TOK].rearrange("p (s t) -> p s t", t=TDEC)))
            pool.wait_ge(st_evac, 2)
            for c in range(2):
                for x, w, z, prompt in ((pe_[:, c], pw, zt[:, c, 0:SEQ].rearrange("p (s t) -> p s t", s=1), True),
                                        (se[:, c], sw, zt[:, c, SEQ:TOK].rearrange("p (s t) -> p s t", t=TDEC), False)):
                    src, lo = x, 0
                    for step in range(2 * c + 2):
                        sh = 1 << step
                        dst = w[step % 2]
                        link(nc.gpsimd.tensor_tensor(dst[:, :, lo + sh:], src[:, :, lo + sh:],
                                                     src[:, :, lo:x.shape[2] - sh], ALU.add))
                        src, lo = dst, lo + sh
                        half = step - 2 * c
                        if half >= 0:
                            r = r64(half)
                            link(nc.gpsimd.tensor_scalar(z[r], dst[r, :, POOL_STATE:], small[r, C_INVW + c:C_INVW + c + 1],
                                                         None, ALU.mult))
                            if prompt:
                                ic = small[r, C_INVC + 16 * c:C_INVC + 16 * c + 16].rearrange("p (s t) -> p s t", s=1)
                                link(nc.gpsimd.tensor_tensor(z[r, :, 0:16], dst[r, :, POOL_STATE:POOL_STATE + 16], ic, ALU.mult))
                    link(nc.gpsimd.tensor_tensor(z, z, x[:, :, POOL_STATE:], ALU.subtract))
            pool.wait_ge(mix_loaded, 16 * (1 + GROUPS))
            pool.sem_inc(z_ready, 1)

        @block.scalar
        def _(act):
            act.wait_ge(st_filled, 1)
            for c in range(2):
                nc.scalar.activation(se[:, c, :, 0:POOL_STATE],
                                     xp[:, c * 128:c * 128 + NSEQ * POOL_STATE].rearrange("p (s t) -> p s t", t=POOL_STATE),
                                     ACT.Copy).then_inc(st_evac, 1)
            act.wait_ge(un_filled, 1)
            for j, w in ((0, P), (1, SMP)):
                nc.scalar.activation(un[:w, :, j, :], xp[:w, 256 * j:256 * j + 256].rearrange("p (c e) -> p c e", c=2),
                                     ACT.Copy).then_inc(un_evac, 1)

            def kq(s, i, b, between, copy_out):
                for m, h in enumerate((0, 2, 4)):
                    if h == 4 and between:
                        between()
                    act.wait_ge(kt_filled[0], s * 3 + m + 1)
                    nc.scalar.activation(kt[b][:, h, 0:PAST], ktp[0][:], ACT.Copy).then_inc(kt_evac[0], 1)
                if copy_out:
                    copy_out()
                act.wait_ge(sm_done, s + 1)
                nc.scalar.activation(s_[b][:], s_[b][:], ACT.Exp, bias=nmax[:, b:b + 1], scale=-1.0,
                                     accum_out=den[:, b:b + 1]).then_inc(ex_done, 1)

            def pv(s, i, b):
                act.wait_ge(pt_filled, s + 1)
                nc.scalar.activation(pts[b][:, 0:4 * SROWS], ptp[:, 0:4 * SROWS], ACT.Copy).then_inc(pt_evac, 1)
                nc.scalar.activation(pts[b][:TDEC, 4 * SROWS:], ptp[:TDEC, 4 * SROWS:5 * SROWS], ACT.Copy).then_inc(pt_evac, 1)

            def out(s, i, b):
                act.wait_ge(pv_done, s + 1)
                if later(s):
                    act.wait_ge(sel_done, s)
                nc.scalar.activation(on[:, 0:ATTW // 2], pvp[0][:SROWS, 0:ATTW // 2], ACT.Copy).then_inc(on_act, 1)
            order(act, kq, pv, out, lambda s, i, b: None, lambda: None)

        @block.vector
        def _(dve):
            dve.wait_ge(zeroed, 3)
            dve.wait_ge(bias_loaded, 16)

            def kq(s, i, b, between, copy_out):
                if later(i):
                    dve.wait_ge(sc_done, s - 1)
                one = slice(s * TDEC, (s + 1) * TDEC) if isinstance(s, int) else bass.ds(s * TDEC, TDEC)
                for a in range(2):
                    nc.vector.tensor_scalar(qb[b][:].rearrange("p (h c) -> p h c", c=112)[r64(a), :, 8 * a:8 * a + 8],
                                            qts[r64(a), :, one], 1.0, None, ALU.mult).then_inc(qb_ready, 1)
                for m, h in enumerate((1, 3, 5)):
                    dve.wait_ge(kt_filled[1], s * 3 + m + 1)
                    nc.vector.tensor_copy(kt[b][:, h, 0:PAST], ktp[1][:]).then_inc(kt_evac[1], 1)
                dve.wait_ge(kn_filled, s + 1)
                nc.vector.tensor_copy(kt[b][:, :, PAST:], xp[:, 0:PAIRS * TDEC].rearrange("p (h t) -> p h t", t=TDEC)).then_inc(kn_evac, 1)
                if copy_out:
                    copy_out()
                dve.wait_ge(sc_done, s + 1)
                nc.vector.tensor_copy(spare[:], small[:SROWS, 0:1])
                nc.vector.tensor_tensor_reduce(out=s_[b][:], in0=scp[:SROWS, 0:KEYS], in1=sbias[:], scale=-1.0, scalar=BIG,
                                               op0=ALU.add, op1=ALU.min, accum_out=nmax[:, b:b + 1]).then_inc(sm_done, 1)
                dve.wait_ge(ex_done, s + 1)
                nc.vector.reciprocal(inv[:, b:b + 1], den[:, b:b + 1]).then_inc(inverted, 1)
                dve.wait_ge(inverted, s + 1)
                nc.vector.tensor_scalar(s_[b][:], s_[b][:], inv[:, b:b + 1], None, ALU.mult).then_inc(pn_done, 1)

            def out(s, i, b):
                dve.wait_ge(pv_done, s + 1)
                if later(s):
                    dve.wait_ge(sel_done, s)
                nc.vector.tensor_copy(on[:, ATTW // 2:], pvp[1][:SROWS, 0:ATTW // 2]).then_inc(on_dve, 1)

            def pick(s, i, b):
                dve.wait_ge(sel_done, s + 1)
                one = slice(s * TDEC, (s + 1) * TDEC) if isinstance(s, int) else bass.ds(s * TDEC, TDEC)
                for a in range(2):
                    nc.vector.tensor_scalar(cats[r64(a), 2:KD, one],
                                            picked[r64(a)].rearrange("p (h c) -> p h c", c=16)[:, :, 8 * a:8 * a + 8],
                                            1.0, None, ALU.mult).then_inc(o_evac, 1)
            def mix():
                dve.wait_ge(mix_loaded, 16 * (1 + GROUPS))
                for u in range(6):
                    c, (t0, n) = u // 3, MIXES[u % 3]
                    dve.wait_ge(mixed, u + 1)
                    dst = cats[:, c, :] if t0 == SEQ else pc[:, c, t0:t0 + n]
                    nc.vector.tensor_scalar(dst, ktp[u % 2][:, 0:n], psc[:, c:c + 1], None, ALU.mult).then_inc(mix_evac, 1)
            order(dve, kq, lambda s, i, b: None, out, pick, mix)

        @block.tensor
        def _(pe):
            pe.wait_ge(state_loaded, 16)
            rows = NSEQ * POOL_STATE
            for c in range(2):
                last = nc.tensor.transpose(xp[:, c * 128:c * 128 + rows], stn[:, c * P:(c + 1) * P], ident[:rows, :rows])
            last.then_inc(st_filled, 1)
            pe.wait_ge(st_evac, 2)
            for c in range(2):
                nc.tensor.transpose(xp[:, c * P:(c + 1) * P], ut[:, c, SEQ - P:SEQ], ident[:])
            for c in range(2):
                last = nc.tensor.transpose(xp[:SMP, 256 + c * P:256 + (c + 1) * P], ut[:, c, SEQ:TOK], ident[:])
            last.then_inc(un_filled, 1)

            def kq(s, i, b, between, copy_out):
                pe.wait_ge(k_loaded[b], i * 32 + 32)

                def turn_keys(h):
                    if later(s) or h >= 2:
                        pe.wait_ge(kt_evac[h % 2], s * 3 + h // 2)
                    for j in range(4):
                        last = nc.tensor.transpose(ktp[h % 2][:, j * P:(j + 1) * P], kc[b][:, j, h * P:(h + 1) * P], ident[:])
                    last.then_inc(kt_filled[h % 2], 1)
                turn_keys(0)
                turn_keys(1)
                pe.wait_ge(qb_ready, s * 2 + 2)
                if later(s):
                    pe.wait_ge(sm_done, s)
                for h in range(PAIRS):
                    if h == 1:
                        if later(s):
                            pe.wait_ge(kn_evac, s)
                        else:
                            pe.wait_ge(un_evac, 2)
                        if later(i):
                            pe.wait_ge(o_evac, s * 2 - 2)
                    if h + 2 < PAIRS:
                        turn_keys(h + 2)
                    if h == 1:
                        for g in range(PAIRS):
                            last = nc.tensor.transpose(xp[:, g * TDEC:(g + 1) * TDEC], kn[b][:, g * P:(g + 1) * P], ident[:TDEC, :TDEC])
                        last.then_inc(kn_filled, 1)
                    if h == 3 and between:
                        between()
                    pe.wait_ge(kt_evac[h % 2], s * 3 + h // 2 + 1)
                    nc.tensor.matmul(scp[:SROWS, 0:PAST], qb[b][:, h * SROWS:(h + 1) * SROWS], kt[b][:, h, 0:PAST],
                                     start=(h == 0), stop=(h == PAIRS - 1))
                pe.wait_ge(kn_evac, s + 1)
                for h in range(PAIRS):
                    last = nc.tensor.matmul(scp[:SROWS, PAST:KEYS], qb[b][:, h * SROWS:(h + 1) * SROWS], kt[b][:, h, PAST:KEYS],
                                            start=(h == 0), stop=(h == PAIRS - 1))
                last.then_inc(sc_done, 1)

            def pv(s, i, b):
                pe.wait_ge(pn_done, s + 1)
                if later(s):
                    pe.wait_ge(pt_evac, s * 2)
                for j in range(4):
                    nc.tensor.transpose(ptp[:, j * SROWS:(j + 1) * SROWS], s_[b][:, j * P:(j + 1) * P], ident[:SROWS, :SROWS])
                nc.tensor.transpose(ptp[:TDEC, 4 * SROWS:5 * SROWS], s_[b][:, PAST:KEYS], ident[:SROWS, :SROWS]).then_inc(pt_filled, 1)
                pe.wait_ge(v_loaded[b], i * 32 + 32)
                pe.wait_ge(pt_evac, s * 2 + 2)
                if later(s):
                    pe.wait_ge(on_act, s)
                    pe.wait_ge(on_dve, s)
                half = ATTW // 2
                for o in range(2):
                    for j in range(5):
                        x, n = (vc[b][:, j, o * half:(o + 1) * half], P) if j < 4 else (vn[b][:, o * half:(o + 1) * half], TDEC)
                        last = nc.tensor.matmul(pvp[o][:SROWS, 0:half], pts[b][:n, j * SROWS:(j + 1) * SROWS], x,
                                                start=(j == 0), stop=(j == 4))
                last.then_inc(pv_done, 1)

            def pick(s, i, b):
                pe.wait_ge(on_act, s + 1)
                pe.wait_ge(on_dve, s + 1)
                if later(s):
                    pe.wait_ge(o_evac, s * 2)
                for h in range(PAIRS):
                    last = nc.tensor.matmul(picked[:, h * 16:(h + 1) * 16], on[:, h * P:(h + 1) * P],
                                            ident[:SROWS, h * 16:(h + 1) * 16], start=True, stop=True)
                last.then_inc(sel_done, 1)
            def mix():
                pe.wait_ge(z_ready, 1)
                for u in range(6):
                    c, (t0, n) = u // 3, MIXES[u % 3]
                    if u >= 2:
                        pe.wait_ge(mix_evac, u - 1)
                    nc.tensor.matmul(ktp[u % 2][:, 0:n], wp[:, c, :], zt[:, c, t0:t0 + n], start=True, stop=True).then_inc(mixed, 1)
            order(pe, kq, pv, lambda s, i, b: None, pick, mix)


LOGITS = GROUPS + EXPERTS


def project_out(nc, d, ident, eps, turn, cats, hid, xfd, h, lg):
    with ExitStack() as ctx:
        sb, ps, sem = tools(nc, ctx)
        WB = 4
        wraw = [sb(f"d_wraw{b}", [P, D]) for b in range(WB)]
        wh, wl = sb("d_wh", [P, KD, D], F32R), sb("d_wl", [P, KD, D], F32R)
        cat = [sb(f"d_cat{b}", [P, KD, P]) for b in range(2)]
        ch = [sb(f"d_ch{b}", [P, KD, P], F32R) for b in range(2)]
        cl = [sb(f"d_cl{b}", [P, KD, P], F32R) for b in range(2)]
        xr = [sb(f"d_x{b}", [P, D]) for b in range(2)]
        xf = [sb(f"d_xf{b}", [P, D]) for b in range(2)]
        xft = sb("d_xft", [P, KD, P])
        junk, gf = sb("d_junk", [P, D]), sb("d_g", [P, D])
        wr, br = sb("d_wr", [P, KD, LOGITS]), sb("d_br", [P, LOGITS])
        ssq, std, rin = ([sb(f"d_{n}{b}", [P, 1]) for b in range(2)] for n in ("ssq", "std", "rin"))
        op = [ps(f"d_op{b}", [P, D]) for b in range(2)]
        xtp = ps("d_xtp", [P, KD, P])
        lgp = ps("d_lgp", [P, 512])
        consts, w_loaded, w_lo = sem("d_consts"), [sem(f"d_w_loaded{b}") for b in range(WB)], sem("d_w_lo")
        w_hi = sem("d_w_hi")
        loaded = [sem(f"d_loaded{b}") for b in range(2)]
        c_hi, c_lo, out_done, h_done, squared, rooted, inverted, xf_done = (
            sem("d_" + n) for n in ("c_hi", "c_lo", "out", "h", "squared", "rooted", "inverted", "xf"))
        turned, t_evac, routed, lg_done = (
            sem("d_" + n) for n in ("turned", "t_evac", "routed", "lg"))
        stored = [sem(f"d_stored{b}") for b in range(2)]
        block = ctx.enter_context(nc.Block())
        w_out = d["w_out"].rearrange("l (k p) c -> p (l k) c", p=P)
        catd = hid.rearrange("(k p) t -> p k t", p=P)
        xp = d["x_prompt"].rearrange("a t d -> (a t) d")
        xs = d["x_sample"].rearrange("a t d -> (a t) d")

        def rows(t, n):
            return slice(t * P, t * P + n) if isinstance(t, int) else bass.ds(t * P, n)

        def h_tile(t, n):
            return (h[:n, t:t + 1, :] if isinstance(t, int) else h[:n, bass.ds(t, 1), :]).rearrange("p a c -> p (a c)")

        def of_next(part, t, i, b):
            if not (isinstance(t, int) and t == QT):
                part(t + 1, i + b, 1 - b, SMP if isinstance(t, int) and t == QT - 1 else P)

        @block.sync
        def _(sp):
            for k in range(KD):
                if k >= WB:
                    sp.wait_ge(w_lo, k - WB + 1)
                sp.dma_start(wraw[k % WB][:], w_out[:, k, :]).then_inc(w_loaded[k % WB], 16)

        @block.gpsimd
        def _(pool):
            def load(t, i, b, n):
                if later(i):
                    pool.wait_ge(c_hi, t - 1)
                    pool.wait_ge(c_lo, t - 1)
                    pool.wait_ge(h_done, t - 1)
                    pool.sem_inc(turn, 1)
                if n == P:
                    pool.dma_start(cat[b][:], catd[:, :, rows(t, P)]).then_inc(loaded[b], 16)
                    pool.dma_start(xr[b][:], xp[rows(t, P), :]).then_inc(loaded[b], 16)
                else:
                    pool.dma_start(xr[b][:n, :], xs).then_inc(loaded[b], 16)
            load(0, 0, 0, P)
            load(1, 0, 1, P)
            pool.dma_start(gf[:], d["g_ffn"].partition_broadcast(P).rearrange("p a d -> p (a d)")).then_inc(consts, 16)
            pool.dma_start(br[:, 0:GROUPS], d["b_router_group"].partition_broadcast(P).rearrange("p a g -> p (a g)")).then_inc(consts, 16)
            pool.dma_start(br[:, GROUPS:], d["b_router_expert"].partition_broadcast(P).rearrange("p a g e -> p (a g e)")).then_inc(consts, 16)
            pool.dma_start(wr[:, :, 0:GROUPS], d["w_router_group"].rearrange("l (k p) g -> p (l k) g", p=P)).then_inc(consts, 16)
            for g in range(GROUPS):
                pool.dma_start(wr[:, :, GROUPS + g * EPG:GROUPS + (g + 1) * EPG],
                               d["w_router_expert"][0, g, :, :].rearrange("(k p) e -> p k e", p=P)).then_inc(consts, 16)
            with pool.Fori(1, QT // 2) as i:
                for b in range(2):
                    load(i * 2 + b, i, b, P)
            load(QT, QT // 2, 0, SMP)

        @block.scalar
        def _(act):
            def split(t, i, b, n):
                if n == P:
                    act.wait_ge(loaded[b], i * 32 + 32)
                if later(i):
                    act.wait_ge(out_done, t - 1)
                src = cat[b][:] if n == P else cats[:]
                nc.scalar.activation(ch[b][:, :, :n], src, ACT.Copy).then_inc(c_hi, 1)

            def project(t, i, b, n):
                of_next(split, t, i, b)
                if not later(t):
                    norm(t, i, b, n)

            def norm(t, i, b, n):
                act.wait_ge(h_done, t + 1)
                nc.scalar.activation(junk[:n, :], h_tile(t, n), ACT.Square, accum_out=ssq[b][:n, :]).then_inc(squared, 1)
                act.wait_ge(squared, t + 1)
                nc.scalar.activation(std[b][:n, :], ssq[b][:n, :], ACT.Sqrt, bias=eps[:n, :], scale=1.0 / D).then_inc(rooted, 1)

            def router(t, i, b, n):
                act.wait_ge(turned, t + 1)
                if later(t):
                    act.wait_ge(routed, t)
                nc.scalar.activation(xft[:, :, :n], xtp[:, :, :n], ACT.Copy).then_inc(t_evac, 1)
                act.wait_ge(xf_done, t + 1)
                act.sem_inc(turn, 1)
                dst = slice(t * P, t * P + n) if isinstance(t, int) else bass.ds(t * P, n)
                act.dma_start(xfd[dst, :], xf[b][:n, :]).then_inc(stored[b], 16)
                of_next(norm, t, i, b)
            split(0, 0, 0, P)
            for k in range(KD):
                act.wait_ge(w_loaded[k % WB], 16 * (k // WB + 1))
                nc.scalar.activation(wh[:, k, :], wraw[k % WB][:], ACT.Copy).then_inc(w_hi, 1)
            two_stages(act, project, router)
            act.wait_ge(stored[0], (QT // 2 + 1) * 16)
            act.wait_ge(stored[1], QT // 2 * 16)

        @block.vector
        def _(dve):
            nc.vector.memset(lg[:], 0.0)

            def split(t, i, b, n):
                dve.wait_ge(c_hi, t + 1)
                src = cat[b][:] if n == P else cats[:]
                nc.vector.tensor_tensor(cl[b][:, :, :n], src, ch[b][:, :, :n].bitcast(F32), ALU.subtract).then_inc(c_lo, 1)

            def project(t, i, b, n):
                of_next(split, t, i, b)
                dve.wait_ge(loaded[b], i * 32 + (32 if n == P else 16))
                if later(i):
                    dve.wait_ge(stored[b], i * 16)
                dve.wait_ge(out_done, t + 1)
                nc.vector.tensor_tensor(h_tile(t, n), op[b][:n, :], xr[b][:n, :], ALU.add).then_inc(h_done, 1)
                dve.wait_ge(rooted, t + 1)
                nc.vector.reciprocal(rin[b][:n, :], std[b][:n, :]).then_inc(inverted, 1)
                dve.wait_ge(inverted, t + 1)
                nc.vector.scalar_tensor_tensor(xf[b][:n, :], h_tile(t, n), rin[b][:n, :], gf[:n, :],
                                               ALU.mult, ALU.mult).then_inc(xf_done, 1)

            def router(t, i, b, n):
                dve.wait_ge(routed, t + 1)
                one = slice(t, t + 1) if isinstance(t, int) else bass.ds(t, 1)
                nc.vector.tensor_tensor(lg[:n, one, :].rearrange("p a l -> p (a l)"), lgp[:n, 0:LOGITS], br[:n, :],
                                        ALU.add).then_inc(lg_done, 1)
            split(0, 0, 0, P)
            for k in range(KD):
                dve.wait_ge(w_hi, k + 1)
                nc.vector.tensor_tensor(wl[:, k, :], wraw[k % WB][:], wh[:, k, :].bitcast(F32), ALU.subtract).then_inc(w_lo, 1)
            dve.wait_ge(consts, 16 * (4 + GROUPS))
            two_stages(dve, project, router)

        @block.tensor
        def _(pe):
            def project(t, i, b, n):
                pe.wait_ge(c_lo, t + 1)
                if later(i):
                    pe.wait_ge(h_done, t - 1)
                for k in range(KD):
                    if k == KD // 2 and later(t):
                        turn_tile(t - 1, 1 - b, P)
                    if not later(t):
                        pe.wait_ge(w_lo, k + 1)
                    for j, (x, w) in enumerate(((ch, wh), (cl, wh), (ch, wl))):
                        for o in range(2):
                            cols = slice(512 * o, 512 * o + 512)
                            last = nc.tensor.matmul(op[b][:n, cols], x[b][:, k, :n], w[:, k, cols],
                                                    start=(k == 0 and j == 0), stop=(k == KD - 1 and j == 2))
                last.then_inc(out_done, 1)

            def turn_tile(t, b, n):
                if later(t):
                    pe.wait_ge(t_evac, t)
                pe.wait_ge(xf_done, t + 1)
                for k in range(KD):
                    last = nc.tensor.transpose(xtp[:, k, :n], xf[b][:n, k * P:(k + 1) * P], ident[:n, :n])
                last.then_inc(turned, 1)

            def router(t, i, b, n):
                if isinstance(t, int) and t == QT:
                    turn_tile(t, b, n)
                if later(t):
                    pe.wait_ge(lg_done, t)
                if isinstance(t, int) and t == 0:
                    pe.wait_ge(consts, 16 * (4 + GROUPS))
                pe.wait_ge(t_evac, t + 1)
                for k in range(KD):
                    last = nc.tensor.matmul(lgp[:n, 0:LOGITS], xft[:, k, :n], wr[:, k, :], start=(k == 0), stop=(k == KD - 1))
                last.then_inc(routed, 1)
            two_stages(pe, project, router)


def route(nc, d, small, turn, lg, gates, slot, jobs, lst, xfd, ins):
    with ExitStack() as ctx:
        sb, ps, sem = tools(nc, ctx)
        tri, ones = sb("e_tri", [P, P]), sb("e_ones", [P, P])
        before = sb("e_before", [P, EXPERTS, EXPERTS])
        tokid = sb("e_tokid", [P, NT], I32)
        gl8, mx8, ix8 = sb("e_gl8", [P, NT, 8]), sb("e_mx8", [P, NT, 8]), sb("e_ix8", [P, NT, 8], U32)
        el8, me8, ie8 = sb("e_el8", [P, NT, 8]), sb("e_me8", [P, NT, 8]), sb("e_ie8", [P, NT, 8], U32)
        g1, i1, i2 = sb("e_g1", [P, NT]), sb("e_i1", [P, NT]), sb("e_i2", [P, NT])
        ex, sm, dv, r = sb("e_ex", [P, NT, GROUPS]), sb("e_sm", [P, NT]), sb("e_dv", [P, NT]), sb("e_r", [P, NT])
        oh, pr = sb("e_oh", [P, NT, GROUPS]), sb("e_pr", [P, NT, GROUPS, EPG])
        ea = [sb(f"e_ea{n}", [P, NT]) for n in range(2)]
        sel = [sb(f"e_sel{n}", [P, NT, EXPERTS]) for n in range(2)]
        m, mp = sb("e_m", [P, NT, EXPERTS]), sb("e_mp", [P, NT + 1, EXPERTS])
        pos, over, base = sb("e_pos", [P, NT, EXPERTS]), sb("e_over", [P, NT, EXPERTS]), sb("e_base", [P, EXPERTS])
        cnt, st, nt = sb("e_cnt", [P, EXPERTS]), sb("e_st", [P, EXPERTS, 11]), sb("e_nt", [P, EXPERTS])
        bm, ob, oi = sb("e_bm", [P, EXPERTS, EXPERTS]), sb("e_ob", [P, EXPERTS]), sb("e_oi", [P, EXPERTS])
        sl, sf = sb("e_sl", [P, NT, EXPERTS]), sb("e_sf", [P, NT])
        jm, jf = sb("e_jm", [1, JOBS, EXPERTS]), sb("e_jf", [1, JOBS + 1])
        pp = ps("e_pp", [P, 512])
        consts, chain, exped, picked, counted, scattered, slots_ready = (
            sem("e_" + n) for n in ("consts", "chain", "exped", "picked", "counted", "scattered", "slots"))
        block = ctx.enter_context(nc.Block())
        V = nc.vector

        def bc(ap, shape):
            return ap.to_broadcast(shape)

        @block.sync
        def _(sp):
            sp.dma_start(tri[:], d["c_tri"]).then_inc(consts, 16)
            sp.dma_start(before[:], d["c_before"].rearrange("p (e f) -> p e f", f=EXPERTS)).then_inc(consts, 16)
            sp.dma_start(tokid[:], d["c_tokid"]).then_inc(consts, 16)
            for r in range(RING):
                load_gate_up(sp, d, ins, r, r)
                load_down(sp, d, ins, r, r)

        exp_in = sem("e_exp_in")

        @block.scalar
        def _(act):
            act.wait_ge(exp_in, 1)
            nc.scalar.activation(ex[:], ex[:], ACT.Exp).then_inc(exped, 1)
            act.wait_ge(exp_in, 2)
            nc.scalar.activation(r[:], dv[:], ACT.Exp).then_inc(exped, 1)

        @block.vector
        def _(dve):
            n = [0]

            def link(ins):
                n[0] += 1
                ins.then_inc(chain, 1)
                dve.wait_ge(chain, n[0])

            def col(off, w):
                return small[:, off:off + w]
            V.memset(ones[:], 1.0)
            link(V.memset(gl8[:], -BIG))
            link(V.tensor_copy(gl8[:, :, 0:GROUPS], lg[:, :, 0:GROUPS]))
            for t in range(NT):
                last = V.max(mx8[:, t, :], gl8[:, t, :])
            link(last)
            for t in range(NT):
                last = V.max_index(ix8[:, t, :], mx8[:, t, :], gl8[:, t, :])
            link(last)
            link(V.tensor_copy(g1[:], ix8[:, :, 0]))
            link(V.tensor_tensor(oh[:], bc(g1[:].unsqueeze(2), [P, NT, GROUPS]),
                                 bc(col(C_IOTA, GROUPS).unsqueeze(1), [P, NT, GROUPS]), ALU.is_equal))
            V.tensor_tensor(ex[:], lg[:, :, 0:GROUPS], bc(mx8[:, :, 0:1], [P, NT, GROUPS]), ALU.subtract).then_inc(exp_in, 1)
            for g in range(GROUPS):
                link(V.tensor_tensor(pr[:, :, g, :], lg[:, :, GROUPS + g * EPG:GROUPS + (g + 1) * EPG],
                                     bc(oh[:, :, g:g + 1], [P, NT, EPG]), ALU.mult))
            link(V.tensor_tensor(pr[:, :, 0, :], pr[:, :, 0, :], pr[:, :, 1, :], ALU.add))
            link(V.tensor_tensor(pr[:, :, 2, :], pr[:, :, 2, :], pr[:, :, 3, :], ALU.add))
            link(V.tensor_tensor(el8[:], pr[:, :, 0, :], pr[:, :, 2, :], ALU.add))
            for t in range(NT):
                last = V.max(me8[:, t, :], el8[:, t, :])
            link(last)
            for t in range(NT):
                last = V.max_index(ie8[:, t, :], me8[:, t, :], el8[:, t, :])
            link(last)
            V.tensor_tensor(dv[:], me8[:, :, 1], me8[:, :, 0], ALU.subtract).then_inc(exp_in, 1)
            link(V.tensor_copy(i1[:], ie8[:, :, 0]))
            link(V.tensor_copy(i2[:], ie8[:, :, 1]))
            for a, i in ((0, i1), (1, i2)):
                link(V.scalar_tensor_tensor(ea[a][:], g1[:], float(EPG), i[:], ALU.mult, ALU.add))
                link(V.tensor_tensor(sel[a][:], bc(ea[a][:].unsqueeze(2), [P, NT, EXPERTS]),
                                     bc(col(C_EXP, EXPERTS).unsqueeze(1), [P, NT, EXPERTS]), ALU.is_equal))
            link(V.tensor_tensor(m[:], sel[0][:], sel[1][:], ALU.add))
            link(V.tensor_tensor(m[:], m[:], bc(col(C_VALID, NT).unsqueeze(2), [P, NT, EXPERTS]), ALU.mult))
            link(V.memset(mp[:, 0, :], 0.0))
            for t in range(NT):
                link(V.tensor_tensor(mp[:, t + 1, :], mp[:, t, :], m[:, t, :], ALU.add))
            dve.sem_inc(picked, 1)
            dve.wait_ge(exped, 2)
            link(V.tensor_reduce(sm[:], ex[:], AX.X, ALU.add))
            link(V.scalar_tensor_tensor(sm[:], r[:], 1.0, sm[:], ALU.add, ALU.mult))
            link(V.reciprocal(gates[:, 0, :], sm[:]))
            link(V.tensor_tensor(gates[:, 1, :], gates[:, 0, :], r[:], ALU.mult))
            dve.wait_ge(counted, 1)
            link(V.tensor_copy(pos[:], pp[:, 0:NT * EXPERTS].rearrange("p (t e) -> p t e", e=EXPERTS)))
            link(V.tensor_copy(cnt[:], pp[:, NT * EXPERTS:(NT + 1) * EXPERTS]))
            link(V.tensor_tensor(st[:], bc(cnt[:].unsqueeze(2), [P, EXPERTS, 11]),
                                 bc(col(C_STEP, 11).unsqueeze(1), [P, EXPERTS, 11]), ALU.is_gt))
            link(V.tensor_reduce(nt[:], st[:], AX.X, ALU.add))
            link(V.tensor_tensor(bm[:], before[:], bc(nt[:].unsqueeze(1), [P, EXPERTS, EXPERTS]), ALU.mult))
            link(V.tensor_reduce(ob[:], bm[:], AX.X, ALU.add))
            link(V.tensor_tensor(oi[:], ob[:], nt[:], ALU.add))
            link(V.scalar_tensor_tensor(base[:], ob[:], float(EXPERTS - 1), col(C_EXP, EXPERTS), ALU.add, ALU.subtract))
            link(V.tensor_scalar(over[:], pos[:], float(CAP), None, ALU.is_ge))
            link(V.tensor_tensor(over[:], over[:], bc(base[:].unsqueeze(1), [P, NT, EXPERTS]), ALU.mult))
            link(V.tensor_tensor(over[:], over[:], bc(col(C_EXP, EXPERTS).unsqueeze(1), [P, NT, EXPERTS]), ALU.add))
            link(V.scalar_tensor_tensor(pos[:], over[:], float(CAP), pos[:], ALU.mult, ALU.add))
            for a in range(2):
                link(V.tensor_tensor(sl[:], sel[a][:], pos[:], ALU.mult))
                link(V.tensor_reduce(sf[:], sl[:], AX.X, ALU.add))
                link(V.tensor_copy(slot[:, a, :], sf[:]))
            dve.sem_inc(slots_ready, 1)
            link(V.tensor_tensor(jm[:], bc(small[0:1, C_JOB:C_JOB + JOBS].unsqueeze(2), [1, JOBS, EXPERTS]),
                                 bc(oi[0:1, :].unsqueeze(1), [1, JOBS, EXPERTS]), ALU.is_ge))
            link(V.tensor_reduce(jf[:, 0:JOBS], jm[:], AX.X, ALU.add))
            link(V.tensor_scalar(jf[:, 0:JOBS], jf[:, 0:JOBS], float(EXPERTS - 1), None, ALU.min))
            link(V.tensor_copy(jf[:, 0:EXPERTS], small[0:1, C_EXP:C_EXP + EXPERTS]))
            link(V.tensor_scalar(jm[:, 0, 0:EXPERTS], small[0:1, C_EXP:C_EXP + EXPERTS], float(RING), oi[0:1, EXPERTS - 1:EXPERTS],
                                 ALU.mult, ALU.is_lt))
            link(V.tensor_reduce(jf[:, JOBS:JOBS + 1], jm[:, 0, 0:EXPERTS], AX.X, ALU.add))
            link(V.tensor_scalar(jf[:, JOBS:JOBS + 1], jf[:, JOBS:JOBS + 1], float(EXPERTS // RING - 1), None, ALU.add))
            link(V.tensor_copy(jobs[0:1, :], jf[:]))

        @block.tensor
        def _(pe):
            pe.wait_ge(consts, 48)
            pe.wait_ge(picked, 1)
            w = NT * EXPERTS
            nc.tensor.matmul(pp[:, 0:w], tri[:], m[:].rearrange("p t e -> p (t e)"), start=True, stop=False)
            nc.tensor.matmul(pp[:, 0:w], ones[:], mp[:, 0:NT, :].rearrange("p t e -> p (t e)"), start=False, stop=True)
            nc.tensor.matmul(pp[:, w:w + EXPERTS], ones[:], mp[:, NT, :], start=True, stop=True).then_inc(counted, 1)

        @block.gpsimd
        def _(pool):
            pool.wait_ge(slots_ready, 1)
            pool.wait_ge(consts, 48)
            for t in range(NT):
                n = P if t < QT else SMP
                for a in range(2):
                    pool.indirect_dma_start(out=lst, out_offset=bass.IndirectOffsetOnAxis(ap=slot[:n, a, t:t + 1].bitcast(U32), axis=0),
                                            in_=tokid[:n, t:t + 1], in_offset=None).then_inc(scattered, 16)
            pool.wait_ge(scattered, NT * 32)
            for r in range(RING):
                load_list(pool, ins, lst, r, r)
            for r in range(RING):
                gather_tokens(pool, ins, xfd, turn, 0, r)


def experts(nc, d, ident, turn, jobs, lst, xfd, yb, ins):
    with ExitStack() as ctx:
        sb, ps, sem = tools(nc, ctx)
        wg, wu, wd, xg = ins.wg, ins.wu, ins.wd, ins.xg
        xt = [sb(f"f_xt{b}", [P, KD, CAP]) for b in range(2)]
        sg = [sb(f"f_sg{b}", [P, 2, CAP]) for b in range(2)]
        ht = [sb(f"f_ht{b}", [P, 2, CAP]) for b in range(2)]
        y = [sb(f"f_y{b}", [CAP, D]) for b in range(2)]
        xtp = [ps(f"f_xtp{b}", [P, 4, P]) for b in range(2)]
        gp, upp = ps("f_gp", [P, 4, P]), ps("f_up", [P, 4, P])
        yp = [ps(f"f_yp{b}", [P, 512]) for b in range(2)]
        w_loaded, wd_loaded, gathered = ins.w_loaded, ins.wd_loaded, ins.gathered
        turned, t_act, t_dve = sem("f_turned"), sem("f_t_act"), sem("f_t_dve")
        up_done, silu_done, h_done, down_done, y_act, y_dve = (
            sem("f_" + n) for n in ("up", "silu", "h", "down", "y_act", "y_dve"))
        stored = [sem(f"f_stored{b}") for b in range(2)]
        block = ctx.enter_context(nc.Block())
        most = JOBS // RING

        def turns(eng):
            return eng.value_load(jobs[0:1, JOBS:JOBS + 1], min_val=EXPERTS // RING - 1, max_val=most - 1)

        def order(eng, gather, up, down):
            i_last = turns(eng)
            gather(0, 0, 0)
            up(0, 0, 0)
            gather(1, 0, 1)
            with eng.Fori(0, i_last) as i:
                for r in range(1, RING + 1):
                    up(i * RING + r, i + r // RING, r % RING)
                    gather(i * RING + (r + 1), i + (r + 1) // RING, (r + 1) % RING)
                    down(i * RING + (r - 1), i, r - 1)
            i = i_last
            for r in range(1, RING):
                up(i * RING + r, i, r)
                if r + 1 < RING:
                    gather(i * RING + (r + 1), i, r + 1)
                down(i * RING + (r - 1), i, r - 1)
            down(i * RING + (RING - 1), i, RING - 1)

        @block.sync
        def _(sp):
            i_last = turns(sp)

            def store(j, b):
                sp.wait_ge(y_act, j + 2)
                sp.wait_ge(y_dve, j + 2)
                sp.sem_inc(turn, 1)
                sp.dma_start(yb[bass.ds(j * CAP, CAP), :], y[b][:]).then_inc(stored[b], 16)
            with sp.Fori(0, i_last) as i:
                for r in range(RING):
                    e = sp.value_load(jobs[0:1, bass.ds(i * RING + (RING + r), 1)], min_val=0, max_val=EXPERTS - 1)
                    sp.wait_ge(up_done, i * RING + r + 1)
                    sp.sem_inc(turn, 1)
                    load_gate_up(sp, d, ins, e, r)
                    sp.wait_ge(down_done, i * RING + r + 1)
                    sp.sem_inc(turn, 1)
                    load_down(sp, d, ins, e, r)
                    store(i * RING + r, r % 2)
            for r in range(RING):
                store(i_last * RING + r, r % 2)
            for b in range(2):
                sp.wait_ge(stored[b], i_last * 32 + 33)
                sp.sem_inc(turn, 1)

        @block.gpsimd
        def _(pool):
            i_last = turns(pool)

            with pool.Fori(1, i_last + 1) as i:
                for r in range(RING):
                    pool.wait_ge(turned, i * RING + (r - RING + 1))
                    pool.sem_inc(turn, 1)
                    load_list(pool, ins, lst, i * RING + r, r)
                    gather_tokens(pool, ins, xfd, turn, i, r)

        @block.scalar
        def _(act):
            def gather(j, i, r):
                act.wait_ge(turned, j + 1)
                nc.scalar.activation(xt[r % 2][:, 0:4, :], xtp[0][:, :, 0:CAP], ACT.Copy).then_inc(t_act, 1)

            def up(j, i, r):
                act.wait_ge(up_done, j + 1)
                nc.scalar.activation(sg[r % 2][:], gp[:, 0:2, 0:CAP], ACT.Silu).then_inc(silu_done, 1)

            def down(j, i, r):
                act.wait_ge(stored[r % 2], i * 32 + (r // 2) * 16 + 1)
                act.wait_ge(down_done, j + 1)
                nc.scalar.activation(y[r % 2][:, 0:512], yp[0][:CAP, :], ACT.Copy).then_inc(y_act, 1)
            order(act, gather, up, down)

        @block.vector
        def _(dve):
            dve.sem_inc(stored[0], 1)
            dve.sem_inc(stored[1], 1)
            dve.sem_inc(y_dve, 1)
            dve.sem_inc(y_act, 1)

            def gather(j, i, r):
                dve.wait_ge(turned, j + 1)
                nc.vector.tensor_copy(xt[r % 2][:, 4:8, :], xtp[1][:, :, 0:CAP]).then_inc(t_dve, 1)

            def up(j, i, r):
                dve.wait_ge(silu_done, j + 1)
                nc.vector.tensor_tensor(ht[r % 2][:], sg[r % 2][:], upp[:, 0:2, 0:CAP], ALU.mult).then_inc(h_done, 1)

            def down(j, i, r):
                dve.wait_ge(stored[r % 2], i * 32 + (r // 2) * 16 + 1)
                dve.wait_ge(down_done, j + 1)
                nc.vector.tensor_copy(y[r % 2][:, 512:D], yp[1][:CAP, :]).then_inc(y_dve, 1)
            order(dve, gather, up, down)

        @block.tensor
        def _(pe):
            def gather(j, i, r):
                pe.wait_ge(gathered[r], i * 16 + 16)
                if not isinstance(j, int) or j >= 1:
                    pe.wait_ge(t_act, j)
                    pe.wait_ge(t_dve, j)
                rows = xg[r][:].rearrange("t (p k) -> t k p", k=KD)
                for k in range(KD):
                    last = nc.tensor.transpose(xtp[k // 4][:, k % 4, 0:CAP], rows[:, k, :], ident[:CAP, :CAP])
                last.then_inc(turned, 1)

            def up(j, i, r):
                pe.wait_ge(w_loaded[r], i * 32 + 32)
                pe.wait_ge(t_act, j + 1)
                pe.wait_ge(t_dve, j + 1)
                if not isinstance(j, int) or j >= 1:
                    pe.wait_ge(h_done, j)
                for w, dst in ((wg, gp), (wu, upp)):
                    cols = w[r][:].rearrange("p k (m c) -> p k c m", c=2)
                    for c in range(2):
                        for k in range(KD):
                            last = nc.tensor.matmul(dst[:, c, 0:CAP], cols[:, k, c, :], xt[r % 2][:, k, :],
                                                    start=(k == 0), stop=(k == KD - 1))
                last.then_inc(up_done, 1)

            def down(j, i, r):
                pe.wait_ge(h_done, j + 1)
                pe.wait_ge(wd_loaded[r], i * 16 + 16)
                pe.wait_ge(y_act, j + 1)
                pe.wait_ge(y_dve, j + 1)
                for o in range(2):
                    for c in range(2):
                        last = nc.tensor.matmul(yp[o][:CAP, :], ht[r % 2][:, c, :], wd[r][:, c, 512 * o:512 * o + 512],
                                                start=(c == 0), stop=(c == 1))
                last.then_inc(down_done, 1)
            order(pe, gather, up, down)


def combine(nc, d, eps, h, gates, slot, yb):
    with ExitStack() as ctx:
        sb, ps, sem = tools(nc, ctx)
        B = 4
        ya = [[sb(f"g_y{a}{b}", [P, D]) for b in range(B)] for a in range(2)]
        s1, s2, out = ([sb(f"g_{n}{b}", [P, D]) for b in range(B)] for n in ("s1", "s2", "o"))
        junk, gf = sb("g_junk", [P, D]), sb("g_g", [P, D])
        ssq, std, rin = ([sb(f"g_{n}{b}", [P, 1]) for b in range(B)] for n in ("ssq", "std", "rin"))
        consts = sem("g_consts")
        y_loaded = [sem(f"g_y_loaded{b}") for b in range(B)]
        added, summed, squared, rooted, inverted, normed = (
            sem("g_" + n) for n in ("added", "summed", "squared", "rooted", "inverted", "normed"))
        stored = [sem(f"g_stored{b}") for b in range(B)]
        block = ctx.enter_context(nc.Block())
        yp = d["o_y_prompt"].rearrange("a t d -> (a t) d")
        ys = d["o_y_sample"].rearrange("a t d -> (a t) d")
        N = [P] * QT + [SMP]

        @block.gpsimd
        def _(pool):
            for t, n in enumerate(N):
                if t >= B:
                    pool.wait_ge(summed, t - B + 1)
                for a in range(2):
                    pool.indirect_dma_start(out=ya[a][t % B][:n, :], out_offset=None, in_=yb,
                                            in_offset=bass.IndirectOffsetOnAxis(ap=slot[:n, a, t:t + 1].bitcast(U32), axis=0)
                                            ).then_inc(y_loaded[t % B], 16)

        @block.sync
        def _(sp):
            sp.dma_start(gf[:], d["g_final"].partition_broadcast(P)).then_inc(consts, 16)

            for t, n in enumerate(N):
                sp.wait_ge(normed, t + 1)
                dst = yp[t * P:(t + 1) * P, :] if t < QT else ys
                sp.dma_start(dst, out[t % B][:n, :]).then_inc(stored[t % B], 16)
            for b in range(B):
                sp.wait_ge(stored[b], len(range(b, NT, B)) * 16)

        @block.scalar
        def _(act):
            for t, n in enumerate(N):
                b = t % B
                act.wait_ge(summed, t + 1)
                nc.scalar.activation(junk[:n, :], s2[b][:n, :], ACT.Square, accum_out=ssq[b][:n, :]).then_inc(squared, 1)
                act.wait_ge(squared, t + 1)
                nc.scalar.activation(std[b][:n, :], ssq[b][:n, :], ACT.Sqrt, bias=eps[:n, :], scale=1.0 / D).then_inc(rooted, 1)

        @block.vector
        def _(dve):
            dve.wait_ge(consts, 16)

            def total(t):
                n, b = N[t], t % B
                dve.wait_ge(y_loaded[b], 32 * (t // B + 1))
                nc.vector.scalar_tensor_tensor(s1[b][:n, :], ya[0][b][:n, :], gates[:n, 0, t:t + 1], h[:n, t, :],
                                               ALU.mult, ALU.add).then_inc(added, 1)
                dve.wait_ge(added, t + 1)
                nc.vector.scalar_tensor_tensor(s2[b][:n, :], ya[1][b][:n, :], gates[:n, 1, t:t + 1], s1[b][:n, :],
                                               ALU.mult, ALU.add).then_inc(summed, 1)

            def norm(t):
                n, b = N[t], t % B
                dve.wait_ge(rooted, t + 1)
                nc.vector.reciprocal(rin[b][:n, :], std[b][:n, :]).then_inc(inverted, 1)
                dve.wait_ge(inverted, t + 1)
                if t >= B:
                    dve.wait_ge(stored[b], 16 * (t // B))
                nc.vector.scalar_tensor_tensor(out[b][:n, :], s2[b][:n, :], rin[b][:n, :], gf[:n, :],
                                               ALU.mult, ALU.mult).then_inc(normed, 1)
            total(0)
            for t in range(1, NT):
                total(t)
                norm(t - 1)
            norm(NT - 1)


_INS = ['x_prompt', 'x_sample', 'cache_k', 'cache_v', 'state_pool', 'g_mix', 'w_in', 'w_pool', 'pool_scale', 'w_out',
        'g_ffn', 'w_router_group', 'b_router_group', 'w_router_expert', 'b_router_expert', 'w_gate', 'w_up', 'w_down',
        'g_final']
_OUTS = [('o_y_prompt', (1, SEQ, D)), ('o_y_sample', (NSEQ, TDEC, D)),
         ('o_k_prompt', (1, 1, SEQ, HEADS, HD)), ('o_v_prompt', (1, 1, SEQ, HEADS, HD)),
         ('o_pool_prompt', (1, 1, POOL_STATE, POOLW)),
         ('o_k_sample', (1, NSEQ, TDEC, HEADS, HD)), ('o_v_sample', (1, NSEQ, TDEC, HEADS, HD)),
         ('o_pool_sample', (1, NSEQ, POOL_STATE, POOLW))]


def kernel(**inputs):
    import concourse.bacc as _bacc
    from concourse.bass_utils import run_bass_kernel_spmd as _run

    nc = _bacc.Bacc("TRN2", target_bir_lowering=False, num_devices=1)
    arrays, d = {}, {}
    for name, a in [(n, np.ascontiguousarray(inputs[n])) for n in _INS] + list(constants().items()):
        arrays[f"in_{name}"] = a
        d[name] = nc.dram_tensor(f"in_{name}", a.shape, mybir.dt.from_np(a.dtype), kind="ExternalInput").ap()
    for name, shape in _OUTS:
        d[name] = nc.dram_tensor(name, shape, F32, kind="ExternalOutput").ap()
    build(nc, d)
    r = _run(nc, [arrays], core_ids=[0])
    return tuple(r.results[0][name] for name, _ in _OUTS)
```

```python
from contextlib import ExitStack

import concourse.bass as bass
import numpy as np
from concourse import mybir

F32 = mybir.dt.float32
F32R = mybir.dt.float32r
I32 = mybir.dt.int32
U32 = mybir.dt.uint32
ALU = mybir.AluOpType
ACT = mybir.ActivationFunctionType
AX = mybir.AxisListType

P = 128
D = 1024
KD = D // P
SEQ = 1024
NSEQ, TDEC = 8, 8
SMP = NSEQ * TDEC
TOK = SEQ + SMP
QT = SEQ // P
NT = QT + 1
PAST = 512
HEADS, HD = 12, 64
PAIRS = HEADS // 2
POOLW = 256
ATTW = HEADS * HD
POOL_STATE = 15
WINDOWS = (2, 4, 8, 16)
GROUPS, EPG, FF = 4, 8, 256
EXPERTS = GROUPS * EPG
EPS = 1e-6
SCALE = HD ** -0.5
MASKED = -1e30
BIG = 3e38

CAP = 96
OVER = (2 * TOK) // CAP
RING = 4
JOBS = -(-(EXPERTS + OVER) // RING) * RING
SLOTS = JOBS * CAP
LISTED = SLOTS + RING * CAP
WB = 4


def multiplicity(delta):
    return ((delta >= 0) & (delta <= 128)).astype(np.float64) \
        + ((delta >= 0) & (delta % 4 == 0) & (delta <= 512)) + ((delta >= 0) & (delta % 16 == 0) & (delta <= 2048))


def slopes():
    def geometric(n):
        start = 2.0 ** (-8.0 / n)
        return [start ** (i + 1) for i in range(n)]
    return np.asarray(geometric(8) + geometric(16)[0::2][:HEADS - 8], np.float64)


def constants():
    f = np.float32
    p = np.arange(P)[:, None]
    delta = p + (SEQ - P) - np.arange(SEQ)[None, :]
    c = multiplicity(delta)
    lnc = np.where(c > 0, np.log(np.maximum(c, 1)), MASKED)
    sl = slopes()
    row = np.arange(HEADS * TDEC)
    head, q = row // TDEC, row % TDEC
    x = np.arange(PAST + TDEC)
    key = np.where(x < PAST, 4 * (x % P) + x // P, x)
    d2 = PAST + q[:, None] - key[None, :]
    c2 = multiplicity(d2)
    sbias = np.where(c2 > 0, np.log(np.maximum(c2, 1)) - sl[head][:, None] * d2, MASKED)
    window = np.asarray(WINDOWS)[(np.arange(POOLW) // 64)].reshape(2, P).T
    cnt = np.minimum(np.arange(16)[None, None, :] + 1, window[:, :, None])
    e = np.arange(EXPERTS)
    small = np.concatenate([
        np.tile(-sl, (P, 1)),
        1.0 / window,
        (1.0 / cnt).reshape(P, 32),
        np.tile(np.arange(8), (P, 1)),
        np.tile(e, (P, 1)),
        np.tile(np.arange(1, 12) * CAP, (P, 1)),
        np.tile(np.arange(JOBS) - EXPERTS, (P, 1)),
    ], axis=1)
    before = (e[None, :] < e[:, None]).astype(f).reshape(1, -1)
    return {
        "c_ident": np.eye(P, dtype=f),
        "c_tri": (p < np.arange(P)[None, :]).astype(f),
        "c_dist": np.maximum(delta, 0).astype(f),
        "c_lnc": lnc.astype(f),
        "c_sbias": sbias.astype(f),
        "c_small": small.astype(f),
        "c_before": np.tile(before, (P, 1)).astype(f),
        "c_tokid": (np.arange(NT)[None, :] * P + p).astype(np.int32),
    }


C_SLOPE, C_INVW, C_INVC, C_IOTA, C_EXP, C_STEP, C_JOB = 0, 12, 14, 46, 54, 86, 97
C_SMALL = C_JOB + JOBS


def build(nc, d):
    hid = nc.dram_tensor("scratch_cat", (D, SEQ), F32, kind="Internal").ap()
    xfd = nc.dram_tensor("scratch_xf", (TOK, D), F32, kind="Internal").ap()
    lst = nc.dram_tensor("scratch_list", (LISTED, 1), I32, kind="Internal").ap()
    yb = nc.dram_tensor("scratch_y", (SLOTS, D), F32, kind="Internal").ap()
    with ExitStack() as whole:
        ident = whole.enter_context(nc.sbuf_tensor("ident", [P, P], F32))
        small = whole.enter_context(nc.sbuf_tensor("small", [P, C_SMALL], F32))
        eps = whole.enter_context(nc.sbuf_tensor("eps", [P, 1], F32))
        turn = whole.enter_context(nc.semaphore("turn"))
        ut = whole.enter_context(nc.sbuf_tensor("ut", [P, 2, TOK], F32))
        qts = whole.enter_context(nc.sbuf_tensor("qts", [P, PAIRS, SMP], F32))
        cats = whole.enter_context(nc.sbuf_tensor("cats", [P, KD, SMP], F32))
        with ExitStack() as mixer:
            xh = mixer.enter_context(nc.sbuf_tensor("xh", [P, KD, TOK], F32R))
            xl = mixer.enter_context(nc.sbuf_tensor("xl", [P, KD, TOK], F32R))
            wraw = [mixer.enter_context(nc.sbuf_tensor(f"wraw{c}", [P, KD, P], F32)) for c in range(3)]
            wh = [mixer.enter_context(nc.sbuf_tensor(f"wh{c}", [P, KD, P], F32R)) for c in range(3)]
            wl = [mixer.enter_context(nc.sbuf_tensor(f"wl{c}", [P, KD, P], F32R)) for c in range(3)]
            raw = [mixer.enter_context(nc.sbuf_tensor(f"raw{n}", [P, SEQ if n == "q" else TOK], F32)) for n in "qkv"]
            norm_in(nc, d, ident, small, eps, xh, xl, wraw, wh, wl, raw, qts, lst)
            attention(nc, d, ident, small, turn, xh, xl, wraw, wh, wl, raw, ut, qts, hid, yb)
        with ExitStack() as moe:
            sb, _, sem = tools(nc, moe)
            lg = sb("lg", [P, NT, GROUPS + EXPERTS])
            gates, slot = sb("gates", [P, 2, NT]), sb("slot", [P, 2, NT], I32)
            jobs = sb("jobs", [P, JOBS + 1], I32)
            gfin, gfin_loaded = sb("gfin", [P, D]), sem("gfin_loaded")
            h = sb("h", [P, NT, D])
            with ExitStack() as out:
                sb, _, sem = tools(nc, out)
                wraw = [sb(f"d_wraw{b}", [P, D]) for b in range(WB)]
                w_loaded = [sem(f"d_w_loaded{b}") for b in range(WB)]
                decode(nc, d, ident, small, ut, qts, cats, hid, wraw, w_loaded)
                project_out(nc, d, ident, eps, turn, cats, hid, xfd, h, lg, wraw, w_loaded)
            with ExitStack() as ring:
                sb, _, sem = tools(nc, ring)
                ins = Inputs()
                ins.wg, ins.wu = ([sb(f"f_{n}{r}", [P, KD, FF]) for r in range(RING)] for n in ("wg", "wu"))
                ins.wd = [sb(f"f_wd{r}", [P, 2, D]) for r in range(RING)]
                ins.idx = [sb(f"f_idx{r}", [CAP, 1], I32) for r in range(RING)]
                ins.xg = [sb(f"f_xg{r}", [CAP, D]) for r in range(RING)]
                ins.w_loaded, ins.wd_loaded, ins.idx_loaded, ins.gathered = (
                    [sem(f"f_{n}{r}") for r in range(RING)] for n in ("w_loaded", "wd_loaded", "idx_loaded", "gathered"))
                route(nc, d, small, lg, gates, slot, jobs, lst, gfin, gfin_loaded, ins)
                experts(nc, d, ident, turn, jobs, lst, xfd, yb, ins)
            combine(nc, d, eps, h, gates, slot, yb, gfin, gfin_loaded)


class Inputs:
    pass


def load_gate_up(eng, d, ins, e, r):
    one = slice(e, e + 1) if isinstance(e, int) else bass.ds(e, 1)
    for dst, name in ((ins.wg, "w_gate"), (ins.wu, "w_up")):
        src = d[name].rearrange("l g e (p k) f -> (l g e) p (k f)", k=KD)
        eng.dma_start(dst[r][:].rearrange("p k f -> p (k f)"), src[one].rearrange("a p f -> p (a f)")).then_inc(ins.w_loaded[r], 16)


def load_down(eng, d, ins, e, r):
    one = slice(e, e + 1) if isinstance(e, int) else bass.ds(e, 1)
    src = d["w_down"].rearrange("l g e (p c) n -> (l g e) p (c n)", c=2)
    eng.dma_start(ins.wd[r][:].rearrange("p c n -> p (c n)"), src[one].rearrange("a p f -> p (a f)")).then_inc(ins.wd_loaded[r], 16)


def load_list(pool, ins, lst, j, r):
    lo = j * CAP
    at = slice(lo, lo + CAP) if isinstance(lo, int) else bass.ds(lo, CAP)
    pool.dma_start(ins.idx[r][:], lst[at, :]).then_inc(ins.idx_loaded[r], 16)


def gather_tokens(pool, ins, xfd, idx, r):
    pool.indirect_dma_start(out=ins.xg[r][:], out_offset=None, in_=xfd,
                            in_offset=bass.IndirectOffsetOnAxis(ap=idx.bitcast(U32), axis=0)).then_inc(ins.gathered[r], 16)


def tools(nc, ctx):
    return (lambda n, s, t=F32: ctx.enter_context(nc.sbuf_tensor(n, s, t)),
            lambda n, s, t=F32: ctx.enter_context(nc.psum_tensor(n, s, t)),
            lambda n: ctx.enter_context(nc.semaphore(n)))


def two_stages(eng, first, second):
    first(0, 0, 0, P)
    first(1, 0, 1, P)
    second(0, 0, 0, P)
    first(2, 1, 0, P)
    second(1, 0, 1, P)
    with eng.Fori(1, QT // 2 - 1) as i:
        first(i * 2 + 1, i, 1, P)
        second(i * 2, i, 0, P)
        first(i * 2 + 2, i + 1, 0, P)
        second(i * 2 + 1, i, 1, P)
    first(QT - 1, QT // 2 - 1, 1, P)
    second(QT - 2, QT // 2 - 1, 0, P)
    first(QT, QT // 2, 0, SMP)
    second(QT - 1, QT // 2 - 1, 1, P)
    second(QT, QT // 2, 0, SMP)


def later(i):
    return not isinstance(i, int) or i > 0


def norm_in(nc, d, ident, small, eps, xh, xl, wraw, wh, wl, raw, qts, lst):
    with ExitStack() as ctx:
        sb, ps, sem = tools(nc, ctx)
        xin = [sb(f"a_x{b}", [P, D]) for b in range(2)]
        xn = [sb(f"a_xn{b}", [P, D]) for b in range(2)]
        junk = sb("a_junk", [P, D])
        gm = sb("a_g", [P, D])
        ssq = [sb(f"a_ssq{b}", [P, 1]) for b in range(2)]
        std = [sb(f"a_std{b}", [P, 1]) for b in range(2)]
        rin = [sb(f"a_rin{b}", [P, 1]) for b in range(2)]
        zero = sb("a_zero", [P, LISTED // P], I32)
        xt = [ps(f"a_xt{b}", [P, KD, P]) for b in range(2)]
        consts, x_loaded = sem("a_consts"), [sem(f"a_loaded{b}") for b in range(2)]
        squared, rooted, inverted, normed = sem("a_squared"), sem("a_rooted"), sem("a_inverted"), sem("a_normed")
        turned, hi_done, lo_done, memsets, listed = sem("a_turned"), sem("a_hi"), sem("a_lo"), sem("a_memsets"), sem("a_listed")
        pj = [ps(f"a_pj{b}", [P, 512]) for b in range(2)]
        w_loaded, w_split = sem("a_w_loaded"), sem("a_w_split")
        projected, unit_evac = sem("a_projected"), sem("a_unit_evac")
        xp = d["x_prompt"].rearrange("a t d -> (a t) d")
        xs = d["x_sample"].rearrange("a t d -> (a t) d")
        w_in = d["w_in"].rearrange("l (k p) c -> p (l k) c", p=P)
        block = ctx.enter_context(nc.Block())

        @block.sync
        def _(sp):
            def load(t, i, b, src, n):
                if later(i):
                    sp.wait_ge(normed, t - 1)
                sp.dma_start(xin[b][:n, :], src).then_inc(x_loaded[b], 16)
            load(0, 0, 0, xp[0:P, :], P)
            load(1, 0, 1, xp[P:2 * P, :], P)
            with sp.Fori(1, QT // 2) as i:
                for b in range(2):
                    load(i * 2 + b, i, b, xp[bass.ds(i * (2 * P) + b * P, P), :], P)
            load(QT, QT // 2, 0, xs, SMP)
            sp.wait_ge(memsets, 2)
            sp.dma_start(lst.rearrange("(p a) b -> p (a b)", p=P), zero[:]).then_inc(listed, 16)
            sp.wait_ge(listed, 16)

        @block.gpsimd
        def _(pool):
            pool.dma_start(gm[:], d["g_mix"].partition_broadcast(P).rearrange("p a d -> p (a d)")).then_inc(consts, 16)
            pool.dma_start(ident[:], d["c_ident"]).then_inc(consts, 16)
            pool.dma_start(small[:], d["c_small"]).then_inc(consts, 16)
            for c in range(3):
                pool.dma_start(wraw[c][:], w_in[:, :, POOLW + c * ATTW:POOLW + c * ATTW + P]).then_inc(w_loaded, 16)
            pool.wait_ge(w_loaded, 48)
            for c in range(3):
                nc.gpsimd.tensor_copy(wh[c][:], wraw[c][:]).then_inc(w_split, 1)
                pool.wait_ge(w_split, 2 * c + 1)
                nc.gpsimd.tensor_tensor(wl[c][:], wraw[c][:], wh[c][:].bitcast(F32), ALU.subtract).then_inc(w_split, 1)

        @block.scalar
        def _(act):
            def norm(t, i, b, n):
                act.wait_ge(x_loaded[b], (i + 1) * 16)
                nc.scalar.activation(junk[:n, :], xin[b][:n, :], ACT.Square, accum_out=ssq[b][:n, :]).then_inc(squared, 1)
                act.wait_ge(squared, t + 1)
                nc.scalar.activation(std[b][:n, :], ssq[b][:n, :], ACT.Sqrt, bias=eps[:n, :], scale=1.0 / D).then_inc(rooted, 1)

            def split(t, i, b, n):
                act.wait_ge(turned, t + 1)
                nc.scalar.activation(xh[:, :, token(t, n)], xt[b][:, :, :n], ACT.Copy).then_inc(hi_done, 1)
            act.wait_ge(memsets, 2)
            nc.scalar.activation(std[0][:], eps[:], ACT.Sqrt)
            two_stages(act, norm, split)

        @block.vector
        def _(dve):
            nc.vector.memset(eps[:], EPS).then_inc(memsets, 1)
            nc.vector.memset(zero[:], 0).then_inc(memsets, 1)
            dve.wait_ge(consts, 48)

            def norm(t, i, b, n):
                dve.wait_ge(rooted, t + 1)
                nc.vector.reciprocal(rin[b][:n, :], std[b][:n, :]).then_inc(inverted, 1)
                dve.wait_ge(inverted, t + 1)
                nc.vector.scalar_tensor_tensor(xn[b][:n, :], xin[b][:n, :], rin[b][:n, :], gm[:n, :],
                                               ALU.mult, ALU.mult).then_inc(normed, 1)

            def split(t, i, b, n):
                dve.wait_ge(hi_done, t + 1)
                nc.vector.tensor_tensor(xl[:, :, token(t, n)], xt[b][:, :, :n],
                                        xh[:, :, token(t, n)].bitcast(F32), ALU.subtract).then_inc(lo_done, 1)
            def evac(m):
                dve.wait_ge(projected, m + 1)
                evac_unit(nc, raw, qts, pj[m % 2], 0, FIRST_UNITS[m]).then_inc(unit_evac, 1)

            def split_evac(t, i, b, n):
                split(t, i, b, n)
                if isinstance(t, int) and t >= NT - 3:
                    evac(t - (NT - 3))
            two_stages(dve, norm, split_evac)
            for m in range(3, len(FIRST_UNITS)):
                evac(m)

        @block.tensor
        def _(pe):
            pe.wait_ge(consts, 48)

            def turn_tile(t, b, n):
                pe.wait_ge(normed, t + 1)
                if not isinstance(t, int) or t >= 2:
                    pe.wait_ge(lo_done, t - 1)
                for k in range(KD):
                    last = nc.tensor.transpose(xt[b][:, k, :n], xn[b][:n, k * P:(k + 1) * P], ident[:n, :n])
                last.then_inc(turned, 1)
            for t in range(4):
                turn_tile(t, t % 2, P)

            def project(m):
                u = FIRST_UNITS[m]
                t0, n = TB[u % 3]
                pe.wait_ge(w_split, 2 * (u // 3) + 2)
                pe.wait_ge(lo_done, -(-(t0 + n) // P))
                if m >= 2:
                    pe.wait_ge(unit_evac, m - 1)
                for q in range(3 * KD):
                    last = product(nc, pj[m % 2], wh, wl, xh, xl, u, q)
                last.then_inc(projected, 1)
            turn_tile(4, 0, P)
            project(0)
            turn_tile(5, 1, P)
            project(1)
            turn_tile(6, 0, P)
            turn_tile(7, 1, P)
            project(2)
            turn_tile(QT, 0, SMP)
            for m in range(3, len(FIRST_UNITS)):
                project(m)


def token(t, n):
    return slice(t * P, t * P + n) if isinstance(t, int) else bass.ds(t * P, n)


TB = [(0, 364), (364, 364), (728, TOK - 728)]
UNIT_STEPS = [[0, 1], [2], [3, 4], [5, 6], [7], [8, 9], [10, 11], [12, 13], [14, 15]]
LAST_STEPS = [[0, 1], [2, 3, 4], [5, 6, 7], [8, 9, 10], [11, 12], [13, 14]]
STEPS = [(a, i) for a in range(2) for i in range(QT)]
NAT = [("k", (0, 4)), ("k", (4, 7)), ("k", (7, 9)), ("v", (0, 4)), ("v", (4, 7)), ("v", (7, 9))]
FILLS = [("nat", x) for x in NAT] + [("p", (s, c)) for s, (a, i) in enumerate(STEPS) for c in range(-(-(i + 1) // 4))] \
    + [("o", 0), ("o", 1)]
NF = len(FILLS) // 2
assert len(FILLS) % 2 == 0
S = len(STEPS)
U = len(UNIT_STEPS)
FIRST_UNITS = [0, 3, 1, 4, 2, 5]
assert len(TB) == 3 and len(FIRST_UNITS) == 6


def product(nc, out, wh, wl, xh, xl, u, q):
    c, (t0, n) = u // 3, TB[u % 3]
    w, x = ((wh, xh), (wl, xh), (wh, xl))[q % 3]
    return nc.tensor.matmul(out[:, 0:n], w[c][:, q // 3, :], x[:, q // 3, t0:t0 + n], start=(q == 0), stop=(q == 3 * KD - 1))


def evac_unit(nc, raw, qts, pj, p, u):
    c, (t0, n) = u // 3, TB[u % 3]
    if c > 0:
        return nc.vector.tensor_copy(raw[c][:, t0:t0 + n], pj[:, 0:n])
    if t0 + n > SEQ:
        col = slice(p, p + 1) if isinstance(p, int) else bass.ds(p, 1)
        nc.vector.tensor_scalar(qts[:, col, :].rearrange("p a t -> p (a t)"), pj[:, SEQ - t0:n], SCALE, None, ALU.mult)
    w = min(n, SEQ - t0)
    return nc.vector.tensor_scalar(raw[0][:, t0:t0 + w], pj[:, 0:w], SCALE, None, ALU.mult)


def attention(nc, d, ident, small, turn, xh, xl, wraw, wh, wl, raw, ut, qts, hid, yb):
    with ExitStack() as ctx:
        sb, ps, sem = tools(nc, ctx)
        qs = [sb(f"b_qs{a}", [P, SEQ], F32R) for a in range(2)]
        kh = [sb(f"b_kh{a}", [P, SEQ], F32R) for a in range(2)]
        kl = [sb(f"b_kl{a}", [P, SEQ], F32R) for a in range(2)]
        bias = [sb(f"b_bias{a}", [P, SEQ]) for a in range(2)]
        dist, lnc = sb("b_dist", [P, SEQ]), sb("b_lnc", [P, SEQ])
        nslope = [sb(f"b_nslope{a}", [P, 1]) for a in range(2)]
        nat = {n: sb(f"b_nat{n}", [P, NT, P]) for n in "kv"}
        sc = [sb(f"b_s{b}", [P, SEQ]) for b in range(2)]
        pt = [sb(f"b_pt{b}", [P, SEQ]) for b in range(2)]
        zero = sb("b_zero", [P, 256])
        onat = sb("b_onat", [P, QT, P])
        otr = sb("b_otr", [P, SEQ])
        nmax, den, inv = sb("b_nmax", [P, 4]), sb("b_den", [P, 4]), sb("b_inv", [P, 4])
        scp = [ps(f"b_scp{b}", [P, SEQ]) for b in range(2)]
        tp = [ps(f"b_tp{b}", [P, 512]) for b in range(2)]
        pj, op = ps("b_pj", [P, 512]), ps("b_op", [P, 512])

        consts = sem("b_consts")
        wraw_loaded = [sem(f"b_wraw_loaded{c}") for c in range(3)]
        w_hi, w_lo = sem("b_w_hi"), sem("b_w_lo")
        proj_done, proj_evac = sem("b_proj_done"), sem("b_proj_evac")
        stk_act = [sem(f"b_stk_act{a}") for a in range(2)]
        stk_dve = [sem(f"b_stk_dve{a}") for a in range(2)]
        stk_pool = [sem(f"b_stk_pool{a}") for a in range(2)]
        slope_cur = sem("b_slope")
        scores_ready, smax_done, exp_done = sem("b_scores"), sem("b_smax"), sem("b_exp")
        filled = [sem(f"b_filled{b}") for b in range(2)]
        evac = [sem(f"b_evac{b}") for b in range(2)]
        pv_done, inverted, o_evac = sem("b_pv"), sem("b_inverted"), sem("b_o_evac")
        kv_out, ot_out = sem("b_kv_out"), sem("b_ot_out")
        zeroed, y_cleared = sem("b_zeroed"), sem("b_y_cleared")
        block = ctx.enter_context(nc.Block())

        w_in = d["w_in"].rearrange("l (k p) c -> p (l k) c", p=P)
        kp, vp = (d[n].rearrange("l b (t p) h e -> p (l b t) (h e)", p=P) for n in ("o_k_prompt", "o_v_prompt"))
        ksm, vsm = (d[n].rearrange("l b t h e -> (l b t) (h e)") for n in ("o_k_sample", "o_v_sample"))

        def chunks(nk):
            return [(c, min(4, nk - 4 * c)) for c in range(-(-nk // 4))]

        @block.sync
        def _(sp):
            sp.dma_start(dist[:], d["c_dist"]).then_inc(consts, 16)
            sp.dma_start(lnc[:], d["c_lnc"]).then_inc(consts, 16)

            def load_w(j, c, col):
                sp.wait_ge(w_lo, j * 3 + c + 1)
                sp.dma_start(wraw[c][:], w_in[:, :, col]).then_inc(wraw_loaded[c], 16)

            def store(p):
                for n in "kv":
                    for bb in range(2):
                        last = max(k // 2 for k in range(6) if k % 2 == bb and NAT[k][0] == n)
                        sp.wait_ge(evac[bb], p * NF + last + 2)
                        sp.sem_inc(turn, 1)
                    big, sml = (kp, ksm) if n == "k" else (vp, vsm)
                    sp.dma_start(big[:, :, cols(p)], nat[n][:, 0:QT, :]).then_inc(kv_out, 16)
                    sp.dma_start(sml[:, cols(p)], nat[n][0:SMP, QT, :]).then_inc(kv_out, 16)
                for bb in range(2):
                    sp.wait_ge(evac[bb], (p + 1) * NF + 1)
                    sp.sem_inc(turn, 1)
                sp.dma_start(hid[rows(p), :], otr[:]).then_inc(ot_out, 16)

            def cols(p):
                return slice(p * P, p * P + P) if isinstance(p, int) else bass.ds(p * P, P)

            def rows(p):
                return slice(POOLW + p * P, POOLW + p * P + P) if isinstance(p, int) else bass.ds(p * P + POOLW, P)

            def wcol(j, c):
                base = POOLW + c * ATTW
                return slice(base + j * P, base + j * P + P) if isinstance(j, int) else bass.ds(j * P + base, P)

            for c in range(3):
                load_w(1, c, wcol(1, c))
            sp.wait_ge(zeroed, 1)
            spare = yb[EXPERTS * CAP:SLOTS, :].rearrange("(p a) (c n) -> p (a c) n", p=P, n=256)
            sp.dma_start(spare, zero[:].unsqueeze(1).to_broadcast([P, spare.shape[1], 256])).then_inc(y_cleared, 16)
            with sp.Fori(0, PAIRS - 2) as p:
                for c in range(3):
                    load_w(p + 2, c, wcol(p + 2, c))
                store(p)
            for c in range(2):
                load_w(PAIRS, c, slice(c * P, c * P + P))
            for p in range(PAIRS - 2, PAIRS):
                store(p)
            sp.wait_ge(y_cleared, 16)
            sp.wait_ge(kv_out, PAIRS * 64 + 1)
            sp.wait_ge(ot_out, PAIRS * 16 + 1)

        @block.gpsimd
        def _(pool):
            pool.sem_inc(w_lo, 6)
            nc.gpsimd.memset(zero[:], 0.0).then_inc(zeroed, 1)
            pool.wait_ge(zeroed, 1)
            pool.wait_ge(consts, 32)

            def split_w(j, c):
                pool.wait_ge(wraw_loaded[c], j * 16)
                pool.wait_ge(proj_done, (j - 1) * U + 3 * c + 3)
                pool.sem_inc(turn, 1)
                nc.gpsimd.tensor_copy(wh[c][:], wraw[c][:]).then_inc(w_hi, 1)
                pool.wait_ge(w_hi, j * 3 + c - 2)
                nc.gpsimd.tensor_tensor(wl[c][:], wraw[c][:], wh[c][:].bitcast(F32), ALU.subtract).then_inc(w_lo, 1)

            def head_part(a, p, before, first=False):
                pool.wait_ge(*before)
                pool.wait_ge(stk_act[a], p * 3 + 2)
                nc.gpsimd.tensor_tensor(kl[a][r64(a), :], raw[1][r64(a), 0:SEQ], kh[a][r64(a), :].bitcast(F32),
                                        ALU.subtract).then_inc(stk_pool[a], 1)
                pool.wait_ge(stk_pool[a], p * 3 + 1)
                nc.gpsimd.tensor_tensor(kl[a][r64(1 - a), :], raw[1][r64(a), 0:SEQ], kh[a][r64(a), :].bitcast(F32),
                                        ALU.subtract).then_inc(stk_pool[a], 1)
                pool.wait_ge(stk_pool[a], p * 3 + 2)
                pool.sem_inc(turn, 1)
                nc.gpsimd.tensor_copy(nslope[a][:], small[:, col1(p, a)]).then_inc(slope_cur, 1)
                pool.wait_ge(slope_cur, p * 4 + 2 * a + 1)
                if not first:
                    pool.wait_ge(smax_done, p * S - S + 8 * a + 8 + 2)
                pool.sem_inc(turn, 1)
                nc.gpsimd.tensor_scalar(bias[a][:], dist[:], nslope[a][:], None, ALU.mult).then_inc(slope_cur, 1)
                pool.wait_ge(slope_cur, p * 4 + 2 * a + 2)
                nc.gpsimd.tensor_tensor(bias[a][:], bias[a][:], lnc[:], ALU.add).then_inc(stk_pool[a], 1)

            def col1(p, a):
                return slice(2 * p + a, 2 * p + a + 1) if isinstance(p, int) else bass.ds(p * 2 + a, 1)

            head_part(0, 0, (w_lo, 3 + 3), first=True)
            for c in range(3):
                split_w(1, c)
            head_part(1, 0, (w_lo, 6 + 3), first=True)

            def body(p, more):
                split_w(p + 2, 0)
                split_w(p + 2, 1)
                head_part(0, p + 1, (w_lo, p * 3 + 6 + 2 + 3))
                if more:
                    split_w(p + 2, 2)
                    head_part(1, p + 1, (w_lo, p * 3 + 9 + 3))
                else:
                    head_part(1, p + 1, (stk_pool[0], p * 3 + 6))
            with pool.Fori(0, PAIRS - 2) as p:
                body(p, True)
            body(PAIRS - 2, False)

        def split_act(act, a, p, part):
            if part == 0:
                nc.scalar.activation(qs[a][r64(a), :], raw[0][r64(a), :], ACT.Copy).then_inc(stk_act[a], 1)
            elif part == 1:
                nc.scalar.activation(kh[a][r64(a), :], raw[1][r64(a), 0:SEQ], ACT.Copy).then_inc(stk_act[a], 1)
            else:
                nc.scalar.activation(kh[a][r64(1 - a), :], raw[1][r64(a), 0:SEQ], ACT.Copy).then_inc(stk_act[a], 1)

        def evac_fill(eng, copy, p, n):
            kind, key = FILLS[n]
            b, m = n % 2, n // 2
            eng.wait_ge(filled[b], p * NF + m + 1)
            if kind == "nat":
                name, (t0, t1) = key
                full = min(t1, QT) - t0
                if t1 > QT:
                    copy(nat[name][:SMP, QT, :], tp[b][:SMP, full * P:(full + 1) * P])
                copy(nat[name][:, t0:t0 + full, :], tp[b][:, 0:full * P].rearrange("p (t c) -> p t c", c=P)).then_inc(evac[b], 1)
            elif kind == "p":
                s, c = key
                w = dict(chunks(STEPS[s][1] + 1))[c] * P
                copy(pt[s % 2][:, 512 * c:512 * c + w], tp[b][:, 0:w]).then_inc(evac[b], 1)
            else:
                copy(otr[:, 512 * key:512 * key + 512], tp[b][:, :]).then_inc(evac[b], 1)

        def step_fills(s, b):
            return [n for n, (kind, key) in enumerate(FILLS) if kind == "p" and key[0] == s and n % 2 == b]

        @block.scalar
        def _(act):
            act.sem_inc(evac[0], 1)
            copy = lambda o, i: nc.scalar.activation(o, i, ACT.Copy)

            def exp(p, s):
                a, i = STEPS[s]
                w = (i + 1) * P
                act.wait_ge(smax_done, p * S + s + 3)
                nc.scalar.activation(sc[s % 2][:, 0:w], sc[s % 2][:, 0:w], ACT.Exp, bias=nmax[:, s % 4:s % 4 + 1],
                                     scale=-1.0, accum_out=den[:, s % 4:s % 4 + 1]).then_inc(exp_done, 1)

            def split_a(p, part):
                if part == 0:
                    act.wait_ge(proj_evac, p * U + 6)
                    if not isinstance(p, int) or p > 0:
                        act.wait_ge(scores_ready, p * S - S + 8 + 1)
                split_act(act, 0, p, part)

            def body(p, last):
                act.wait_ge(kv_out, p * 64 + 1)
                act.wait_ge(pv_done, p * S + 2)
                for n in (0, 2, 4):
                    evac_fill(act, copy, p, n)
                exp(p, 0)
                act.wait_ge(scores_ready, p * S + 1)
                split_act(act, 1, p, 0)
                for s in range(S):
                    act.wait_ge(pv_done, p * S + s + 1)
                    for n in step_fills(s, 0):
                        evac_fill(act, copy, p, n)
                    if s + 1 < S:
                        exp(p, s + 1)
                    if s < 2:
                        split_act(act, 1, p, s + 1)
                    if not last and 10 <= s < 13:
                        split_a(p + 1, s - 10)
                act.wait_ge(ot_out, p * 16 + 1)
                evac_fill(act, copy, p, len(FILLS) - 2)
            nc.scalar.activation(den[:, 0:1], small[:, 0:1], ACT.Exp)
            for part in range(3):
                split_a(0, part)
            with act.Fori(0, PAIRS - 1) as p:
                body(p, False)
            body(PAIRS - 1, True)

        @block.vector
        def _(dve):
            dve.sem_inc(evac[1], 1)
            dve.sem_inc(smax_done, 2)
            dve.sem_inc(o_evac, 1)
            dve.sem_inc(kv_out, 1)
            dve.sem_inc(ot_out, 1)
            dve.sem_inc(proj_evac, len(FIRST_UNITS))
            copy = nc.vector.tensor_copy

            def wait_scores(p, s):
                if s in (0, 8):
                    dve.wait_ge(stk_pool[STEPS[s][0]], p * 3 + 3)
                dve.wait_ge(scores_ready, p * S + s + 2)

            def out_evac(p, s):
                a, i = STEPS[s]
                nc.vector.tensor_scalar(onat[:, i, 64 * a:64 * a + 64], op[:, 0:HD], inv[:, s % 4:s % 4 + 1], None,
                                        ALU.mult).then_inc(o_evac, 1)

            def smax(p, s):
                a, i = STEPS[s]
                w = (i + 1) * P
                nc.vector.tensor_tensor_reduce(
                    out=sc[s % 2][:, 0:w], in0=scp[s % 2][:, 0:w], in1=bias[a][:, SEQ - w:SEQ], scale=-1.0, scalar=BIG,
                    op0=ALU.add, op1=ALU.min, accum_out=nmax[:, s % 4:s % 4 + 1]).then_inc(smax_done, 1)

            def evac_proj(p, u, kind="qkv"):
                c, (t0, n) = u // 3, TB[u % 3]
                dve.wait_ge(proj_done, p * U + u + 1)
                if kind == "u":
                    nc.vector.tensor_copy(ut[:, c, t0:t0 + n], pj[:, 0:n]).then_inc(proj_evac, 1)
                else:
                    if u == 3 and (not isinstance(p, int) or p > 0):
                        dve.wait_ge(stk_pool[1], p * 3 - 1)
                        dve.wait_ge(stk_act[1], p * 3)
                    evac_unit(nc, raw, qts, pj, p, u).then_inc(proj_evac, 1)

            def q_lo(a, p):
                dve.wait_ge(stk_act[a], p * 3 + 1)
                nc.vector.tensor_tensor(qs[a][r64(1 - a), :], raw[0][r64(a), :], qs[a][r64(a), :].bitcast(F32),
                                        ALU.subtract).then_inc(stk_dve[a], 1)

            def body(p, last):
                dve.wait_ge(kv_out, p * 64 + 1)
                evac_fill(dve, copy, p, 1)
                wait_scores(p, 0)
                evac_fill(dve, copy, p, 3)
                smax(p, 0)
                dve.wait_ge(scores_ready, p * S + 3)
                evac_fill(dve, copy, p, 5)
                for s in range(S):
                    a, i = STEPS[s]
                    if s + 1 < S:
                        if s >= 1:
                            dve.wait_ge(inverted, p * S + s)
                            wait_scores(p, s + 1)
                            out_evac(p, s - 1)
                        smax(p, s + 1)
                    for n in step_fills(s, 1):
                        evac_fill(dve, copy, p, n)
                    for u, steps in enumerate(LAST_STEPS if last else UNIT_STEPS):
                        if steps[-1] == s:
                            evac_proj(p + 1, u, "u" if last else "qkv")
                    if s == 0:
                        q_lo(1, p)
                    dve.wait_ge(exp_done, p * S + s + 1)
                    nc.vector.reciprocal(inv[:, s % 4:s % 4 + 1], den[:, s % 4:s % 4 + 1]).then_inc(inverted, 1)
                    if s >= S - 2:
                        dve.wait_ge(inverted, p * S + s + 1)
                        dve.wait_ge(pv_done, p * S + s + 3)
                        out_evac(p, s)
                    if not last and s == 12:
                        q_lo(0, p + 1)
                dve.wait_ge(ot_out, p * 16 + 1)
                evac_fill(dve, copy, p, len(FILLS) - 1)
            q_lo(0, 0)
            for u in range(len(FIRST_UNITS), U):
                evac_proj(0, u)
            with dve.Fori(0, PAIRS - 1) as p:
                body(p, False)
            body(PAIRS - 1, True)

        @block.tensor
        def _(pe):
            pe.sem_inc(scores_ready, 1)
            pe.sem_inc(pv_done, 2)
            pe.sem_inc(proj_done, len(FIRST_UNITS))

            def project(j, u, part, parts):
                c = u // 3
                if part == 0:
                    pe.wait_ge(w_lo, j * 3 + c + 1 + 3)
                    if u or not isinstance(j, int) or j > 0:
                        pe.wait_ge(proj_evac, j * U + u)
                for q in range(3 * KD * part // parts, 3 * KD * (part + 1) // parts):
                    last = product(nc, pj, wh, wl, xh, xl, u, q)
                if part == parts - 1:
                    last.then_inc(proj_done, 1)

            def take_bank(p, n):
                pe.wait_ge(evac[n % 2], p * NF + n // 2 + 1)

            def scores(p, s):
                a, i = STEPS[s]
                if s in (0, 8):
                    pe.wait_ge(stk_act[a], p * 3 + 3)
                    pe.wait_ge(stk_dve[a], p + 1)
                    pe.wait_ge(stk_pool[a], p * 3 + 2)
                pe.wait_ge(smax_done, p * S + s + 1)
                for c, m in chunks(i + 1):
                    o = scp[s % 2][:, 512 * c:512 * c + m * P]
                    q = qs[a][:, i * P:(i + 1) * P]
                    nc.tensor.matmul(o, q, kh[a][:, 512 * c:512 * c + m * P], start=True, stop=False)
                    last = nc.tensor.matmul(o, q, kl[a][:, 512 * c:512 * c + m * P], start=False, stop=True)
                last.then_inc(scores_ready, 1)

            def body(p, last_pair):
                pe.wait_ge(proj_evac, p * U + U)
                for n in range(6):
                    name, (t0, t1) = NAT[n]
                    take_bank(p, n)
                    for t in range(t0, t1):
                        w = SMP if t == QT else P
                        last = nc.tensor.transpose(tp[n % 2][:w, (t - t0) * P:(t - t0 + 1) * P],
                                                   raw[1 if name == "k" else 2][:, t * P:t * P + w], ident[:])
                    last.then_inc(filled[n % 2], 1)
                    if n in (1, 3):
                        scores(p, n // 2)
                for s in range(S):
                    a, i = STEPS[s]
                    if 0 < s < S - 1:
                        scores(p, s + 1)
                    pe.wait_ge(exp_done, p * S + s + 1)
                    for c, m in chunks(i + 1):
                        n = FILLS.index(("p", (s, c)))
                        take_bank(p, n)
                        for j in range(m):
                            last = nc.tensor.transpose(tp[n % 2][:, j * P:(j + 1) * P],
                                                       sc[s % 2][:, (4 * c + j) * P:(4 * c + j + 1) * P], ident[:])
                        last.then_inc(filled[n % 2], 1)
                    for u, steps in enumerate(LAST_STEPS if last_pair else UNIT_STEPS):
                        for part, st in enumerate(steps):
                            if st == s:
                                project(p + 1, u, part, len(steps))
                    for b in range(2):
                        mine = step_fills(s, b)
                        if mine:
                            pe.wait_ge(evac[b], p * NF + mine[-1] // 2 + 2)
                    if s == 0:
                        for b in range(2):
                            pe.wait_ge(evac[b], p * NF + 3 + 1)
                    pe.wait_ge(o_evac, p * S + s + 1)
                    for j in range(i + 1):
                        last = nc.tensor.matmul(op[:, 0:HD], pt[s % 2][:, j * P:(j + 1) * P],
                                                nat["v"][:, j, HD * a:HD * a + HD], start=(j == 0), stop=(j == i))
                    last.then_inc(pv_done, 1)
                pe.wait_ge(o_evac, p * S + S + 1)
                for n in (len(FILLS) - 2, len(FILLS) - 1):
                    take_bank(p, n)
                    for j in range(4):
                        t = 4 * FILLS[n][1] + j
                        last = nc.tensor.transpose(tp[n % 2][:, j * P:(j + 1) * P], onat[:, t, :], ident[:])
                    last.then_inc(filled[n % 2], 1)
            for u in range(len(FIRST_UNITS), U):
                project(0, u, 0, 1)
            with pe.Fori(0, PAIRS - 1) as p:
                body(p, False)
            body(PAIRS - 1, True)


def r64(a):
    return slice(64 * a, 64 * a + 64)


KEYS = PAST + TDEC
SROWS = HEADS * TDEC
MIXES = [(0, 512), (512, 512), (SEQ, SMP)]


def decode(nc, d, ident, small, ut, qts, cats, hid, wraw, w_loaded):
    with ExitStack() as ctx:
        sb, ps, sem = tools(nc, ctx)
        kc = [sb(f"c_k{b}", [P, 4, ATTW]) for b in range(2)]
        vc = [sb(f"c_v{b}", [P, 4, ATTW]) for b in range(2)]
        kn = [sb(f"c_kn{b}", [TDEC, ATTW]) for b in range(2)]
        vn = [sb(f"c_vn{b}", [TDEC, ATTW]) for b in range(2)]
        kt = [sb(f"c_kt{b}", [P, PAIRS, KEYS]) for b in range(2)]
        qb = [sb(f"c_qb{b}", [P, PAIRS * 112]) for b in range(2)]
        sbias = sb("c_bias", [SROWS, KEYS])
        s_ = [sb(f"c_s{b}", [SROWS, KEYS]) for b in range(2)]
        pts = [sb(f"c_pt{b}", [P, 5 * SROWS]) for b in range(2)]
        nmax, den, inv = sb("c_nmax", [SROWS, 2]), sb("c_den", [SROWS, 2]), sb("c_inv", [SROWS, 2])
        spare = sb("c_spare", [SROWS, 1])
        ktp = [ps(f"c_ktp{b}", [P, 512]) for b in range(2)]
        on = sb("c_on", [SROWS, ATTW])
        scp = ps("c_scp", [P, 2 * 512])
        pvp = [ps(f"c_pvp{o}", [P, 512]) for o in range(2)]
        ptp, xp = ps("c_ptp", [P, 512]), ps("c_xp", [P, 512])
        picked = xp[:, P:P + PAIRS * 16]
        pe_ = sb("c_pe", [P, 2, 1, POOL_STATE + SEQ])
        se = sb("c_se", [P, 2, NSEQ, POOL_STATE + TDEC])
        pw = [sb(f"c_pw{n}", [P, 1, POOL_STATE + SEQ]) for n in range(2)]
        sw = [sb(f"c_sw{n}", [P, NSEQ, POOL_STATE + TDEC]) for n in range(2)]
        zt = sb("c_zt", [P, 2, TOK])
        wp = sb("c_wp", [P, 2, P])
        psc = sb("c_psc", [P, 2])
        pc = pe_[:, :, 0, 0:SEQ]
        stn = sb("c_stn", [NSEQ * POOL_STATE, POOLW])
        un = sb("c_un", [P, 2, 2, P])

        state_loaded, bias_loaded, mix_loaded = sem("c_state"), sem("c_bias_loaded"), sem("c_mix_loaded")
        k_loaded, v_loaded = ([sem(f"c_{n}_loaded{b}") for b in range(2)] for n in "kv")
        qb_ready = sem("c_qb_ready")
        kt_filled, kt_evac = [sem(f"c_kt_filled{b}") for b in range(2)], [sem(f"c_kt_evac{b}") for b in range(2)]
        kn_filled, kn_evac = sem("c_kn_filled"), sem("c_kn_evac")
        sc_done, sm_done, ex_done, inverted, pn_done = (sem("c_" + n) for n in ("scores", "smax", "exp", "inv", "norm"))
        pt_filled, pt_evac, pv_done, on_act, on_dve, sel_done, o_evac = (
            sem("c_" + n) for n in ("pt_filled", "pt_evac", "pv", "on_act", "on_dve", "sel_done", "o_evac"))
        st_filled, st_evac, un_filled, un_evac = (sem("c_" + n) for n in ("st_filled", "st_evac", "un_filled", "un_evac"))
        pooling, zeroed, z_ready, mixed, mix_evac = (sem("c_" + n) for n in ("pooling", "zeroed", "z_ready", "mixed", "mix_evac"))
        out = sem("c_out")
        block = ctx.enter_context(nc.Block())
        ck, cv = (d[n].rearrange("l s (p j) h e -> (l s) p j (h e)", j=4) for n in ("cache_k", "cache_v"))
        nk, nv = (d[n].rearrange("l s t h e -> (l s) t (h e)") for n in ("o_k_sample", "o_v_sample"))

        def order(eng, kq, pv, out, pick, mix):
            def step(s, i, b, s1, i1, b1):
                kq(s1, i1, b1, lambda part: pv(s, i, b, part), lambda: out(s, i, b))
                pick(s, i, b)
            kq(0, 0, 0, None, None)
            step(0, 0, 0, 1, 0, 1)
            step(1, 0, 1, 2, 1, 0)
            with eng.Fori(1, NSEQ // 2 - 1) as i:
                step(i * 2, i, 0, i * 2 + 1, i, 1)
                step(i * 2 + 1, i, 1, i * 2 + 2, i + 1, 0)
            step(NSEQ - 2, NSEQ // 2 - 1, 0, NSEQ - 1, NSEQ // 2 - 1, 1)
            mix()
            pv(NSEQ - 1, NSEQ // 2 - 1, 1, 0)
            pv(NSEQ - 1, NSEQ // 2 - 1, 1, 1)
            out(NSEQ - 1, NSEQ // 2 - 1, 1)
            pick(NSEQ - 1, NSEQ // 2 - 1, 1)

        @block.sync
        def _(sp):
            def one(s):
                return slice(s, s + 1) if isinstance(s, int) else bass.ds(s, 1)

            def load_k(s, i, b):
                if later(i):
                    sp.wait_ge(sc_done, s - 1)
                sp.dma_start(kc[b][:], ck[one(s), :, :, :].rearrange("a p j c -> p (a j) c")).then_inc(k_loaded[b], 16)
                sp.dma_start(kn[b][:], nk[one(s), :, :].rearrange("a t c -> t (a c)")).then_inc(k_loaded[b], 16)

            def load_v(s, i, b):
                if later(i):
                    sp.wait_ge(pv_done, s - 1)
                sp.dma_start(vc[b][:], cv[one(s), :, :, :].rearrange("a p j c -> p (a j) c")).then_inc(v_loaded[b], 16)
                sp.dma_start(vn[b][:], nv[one(s), :, :].rearrange("a t c -> t (a c)")).then_inc(v_loaded[b], 16)
            sp.dma_start(stn[:], d["state_pool"].rearrange("l s t c -> (l s t) c")).then_inc(state_loaded, 16)
            load_k(0, 0, 0)
            sp.dma_start(sbias[:], d["c_sbias"]).then_inc(bias_loaded, 16)
            load_k(1, 0, 1)
            load_v(0, 0, 0)
            load_v(1, 0, 1)
            with sp.Fori(1, NSEQ // 2) as i:
                for b in range(2):
                    load_k(i * 2 + b, i, b)
                    load_v(i * 2 + b, i, b)
            for k in range(WB):
                load_w_out(sp, d, wraw, w_loaded, k)
            pp, psm = d["o_pool_prompt"], d["o_pool_sample"]
            sp.wait_ge(un_evac, 2)
            sp.dma_start(pp.rearrange("l b t (c p) -> (l b t) c p", c=2), un[P - POOL_STATE:P, :, 0, :]).then_inc(out, 16)
            n_old = POOL_STATE - TDEC
            sp.dma_start(psm[0, :, 0:n_old, :], d["state_pool"][0, :, TDEC:POOL_STATE, :]).then_inc(out, 16)
            for s in range(NSEQ):
                sp.dma_start(psm[0, s, n_old:POOL_STATE, :].rearrange("t (c p) -> t c p", c=2),
                             un[s * TDEC:(s + 1) * TDEC, :, 1, :]).then_inc(out, 16)
            sp.wait_ge(mix_evac, 6)
            sp.dma_start(hid[0:POOLW, :].rearrange("(c p) t -> p c t", p=P), pc).then_inc(out, 16)
            sp.wait_ge(out, (3 + NSEQ) * 16)

        @block.gpsimd
        def _(pool):
            nc.gpsimd.memset(wp[:], 0.0).then_inc(zeroed, 1)
            nc.gpsimd.memset(qb[0][:], 0.0).then_inc(zeroed, 1)
            nc.gpsimd.memset(qb[1][:], 0.0).then_inc(zeroed, 1)
            pool.wait_ge(zeroed, 3)
            pool.dma_start(psc[:], d["pool_scale"].rearrange("l (c p) -> p (l c)", p=P), allow_slow_non_contiguous=True).then_inc(mix_loaded, 16)
            for g in range(GROUPS):
                a = g % 2
                pool.dma_start(wp[r64(a), g // 2, r64(a)], d["w_pool"][0, g, :, :]).then_inc(mix_loaded, 16)
            n = [0]

            def link(ins):
                n[0] += 1
                ins.then_inc(pooling, 1)
                pool.wait_ge(pooling, n[0])
            link(nc.gpsimd.memset(pe_[:, :, :, 0:POOL_STATE], 0.0))
            link(nc.gpsimd.tensor_copy(pe_[:, :, 0, POOL_STATE:], ut[:, :, 0:SEQ]))
            for c in range(2):
                link(nc.gpsimd.tensor_copy(se[:, c, :, POOL_STATE:], ut[:, c, SEQ:TOK].rearrange("p (s t) -> p s t", t=TDEC)))
            pool.wait_ge(st_evac, 2)
            for c in range(2):
                for x, w, z, prompt in ((pe_[:, c], pw, zt[:, c, 0:SEQ].rearrange("p (s t) -> p s t", s=1), True),
                                        (se[:, c], sw, zt[:, c, SEQ:TOK].rearrange("p (s t) -> p s t", t=TDEC), False)):
                    src, lo = x, 0
                    for step in range(2 * c + 2):
                        sh = 1 << step
                        dst = w[step % 2]
                        link(nc.gpsimd.tensor_tensor(dst[:, :, lo + sh:], src[:, :, lo + sh:],
                                                     src[:, :, lo:x.shape[2] - sh], ALU.add))
                        src, lo = dst, lo + sh
                        half = step - 2 * c
                        if half >= 0:
                            r = r64(half)
                            link(nc.gpsimd.tensor_scalar(z[r], dst[r, :, POOL_STATE:], small[r, C_INVW + c:C_INVW + c + 1],
                                                         None, ALU.mult))
                            if prompt:
                                ic = small[r, C_INVC + 16 * c:C_INVC + 16 * c + 16].rearrange("p (s t) -> p s t", s=1)
                                link(nc.gpsimd.tensor_tensor(z[r, :, 0:16], dst[r, :, POOL_STATE:POOL_STATE + 16], ic, ALU.mult))
                    link(nc.gpsimd.tensor_tensor(z, z, x[:, :, POOL_STATE:], ALU.subtract))
            pool.wait_ge(mix_loaded, 16 * (1 + GROUPS))
            pool.sem_inc(z_ready, 1)

        @block.scalar
        def _(act):
            act.wait_ge(st_filled, 1)
            for c in range(2):
                nc.scalar.activation(se[:, c, :, 0:POOL_STATE],
                                     xp[:, c * 128:c * 128 + NSEQ * POOL_STATE].rearrange("p (s t) -> p s t", t=POOL_STATE),
                                     ACT.Copy).then_inc(st_evac, 1)
            act.wait_ge(un_filled, 1)
            for j, w in ((0, P), (1, SMP)):
                nc.scalar.activation(un[:w, :, j, :], xp[:w, 256 * j:256 * j + 256].rearrange("p (c e) -> p c e", c=2),
                                     ACT.Copy).then_inc(un_evac, 1)

            def kq(s, i, b, between, copy_out):
                for m, h in enumerate((0, 2, 4)):
                    if h == 4 and between:
                        between(0)
                    act.wait_ge(kt_filled[0], s * 3 + m + 1)
                    nc.scalar.activation(kt[b][:, h, 0:PAST], ktp[0][:], ACT.Copy).then_inc(kt_evac[0], 1)
                if copy_out:
                    copy_out()
                act.wait_ge(sm_done, s + 1)
                nc.scalar.activation(s_[b][:], s_[b][:], ACT.Exp, bias=nmax[:, b:b + 1], scale=-1.0,
                                     accum_out=den[:, b:b + 1]).then_inc(ex_done, 1)

            def pv(s, i, b, part):
                if part == 1:
                    return
                act.wait_ge(pt_filled, s + 1)
                nc.scalar.activation(pts[b][:, 0:4 * SROWS], ptp[:, 0:4 * SROWS], ACT.Copy).then_inc(pt_evac, 1)
                nc.scalar.activation(pts[b][:TDEC, 4 * SROWS:], ptp[:TDEC, 4 * SROWS:5 * SROWS], ACT.Copy).then_inc(pt_evac, 1)

            def out(s, i, b):
                act.wait_ge(pv_done, s + 1)
                if later(s):
                    act.wait_ge(sel_done, s)
                nc.scalar.activation(on[:, 0:ATTW // 2], pvp[0][:SROWS, 0:ATTW // 2], ACT.Copy).then_inc(on_act, 1)
            order(act, kq, pv, out, lambda s, i, b: None, lambda: None)

        @block.vector
        def _(dve):
            dve.wait_ge(zeroed, 3)
            dve.wait_ge(bias_loaded, 16)

            def kq(s, i, b, between, copy_out):
                if later(i):
                    dve.wait_ge(sc_done, s - 1)
                one = slice(s * TDEC, (s + 1) * TDEC) if isinstance(s, int) else bass.ds(s * TDEC, TDEC)
                for a in range(2):
                    nc.vector.tensor_scalar(qb[b][:].rearrange("p (h c) -> p h c", c=112)[r64(a), :, 8 * a:8 * a + 8],
                                            qts[r64(a), :, one], 1.0, None, ALU.mult).then_inc(qb_ready, 1)
                for m, h in enumerate((1, 3, 5)):
                    dve.wait_ge(kt_filled[1], s * 3 + m + 1)
                    nc.vector.tensor_copy(kt[b][:, h, 0:PAST], ktp[1][:]).then_inc(kt_evac[1], 1)
                dve.wait_ge(kn_filled, s + 1)
                nc.vector.tensor_copy(kt[b][:, :, PAST:], xp[:, 0:PAIRS * TDEC].rearrange("p (h t) -> p h t", t=TDEC)).then_inc(kn_evac, 1)
                if copy_out:
                    copy_out()
                dve.wait_ge(sc_done, s + 1)
                nc.vector.tensor_copy(spare[:], small[:SROWS, 0:1])
                nc.vector.tensor_tensor_reduce(out=s_[b][:], in0=scp[:SROWS, 0:KEYS], in1=sbias[:], scale=-1.0, scalar=BIG,
                                               op0=ALU.add, op1=ALU.min, accum_out=nmax[:, b:b + 1]).then_inc(sm_done, 1)
                dve.wait_ge(ex_done, s + 1)
                nc.vector.reciprocal(inv[:, b:b + 1], den[:, b:b + 1]).then_inc(inverted, 1)
                dve.wait_ge(inverted, s + 1)
                nc.vector.tensor_scalar(s_[b][:], s_[b][:], inv[:, b:b + 1], None, ALU.mult).then_inc(pn_done, 1)

            def out(s, i, b):
                dve.wait_ge(pv_done, s + 1)
                if later(s):
                    dve.wait_ge(sel_done, s)
                nc.vector.tensor_copy(on[:, ATTW // 2:], pvp[1][:SROWS, 0:ATTW // 2]).then_inc(on_dve, 1)

            def pick(s, i, b):
                dve.wait_ge(sel_done, s + 1)
                one = slice(s * TDEC, (s + 1) * TDEC) if isinstance(s, int) else bass.ds(s * TDEC, TDEC)
                for a in range(2):
                    nc.vector.tensor_scalar(cats[r64(a), 2:KD, one],
                                            picked[r64(a)].rearrange("p (h c) -> p h c", c=16)[:, :, 8 * a:8 * a + 8],
                                            1.0, None, ALU.mult).then_inc(o_evac, 1)
            def mix():
                dve.wait_ge(mix_loaded, 16 * (1 + GROUPS))
                for u in range(6):
                    c, (t0, n) = u // 3, MIXES[u % 3]
                    dve.wait_ge(mixed, u + 1)
                    dst = cats[:, c, :] if t0 == SEQ else pc[:, c, t0:t0 + n]
                    nc.vector.tensor_scalar(dst, ktp[u % 2][:, 0:n], psc[:, c:c + 1], None, ALU.mult).then_inc(mix_evac, 1)
            order(dve, kq, lambda s, i, b, part: None, out, pick, mix)

        @block.tensor
        def _(pe):
            pe.wait_ge(state_loaded, 16)
            rows = NSEQ * POOL_STATE
            for c in range(2):
                last = nc.tensor.transpose(xp[:, c * 128:c * 128 + rows], stn[:, c * P:(c + 1) * P], ident[:rows, :rows])
            last.then_inc(st_filled, 1)
            pe.wait_ge(st_evac, 2)
            for c in range(2):
                nc.tensor.transpose(xp[:, c * P:(c + 1) * P], ut[:, c, SEQ - P:SEQ], ident[:])
            for c in range(2):
                last = nc.tensor.transpose(xp[:SMP, 256 + c * P:256 + (c + 1) * P], ut[:, c, SEQ:TOK], ident[:])
            last.then_inc(un_filled, 1)

            def kq(s, i, b, between, copy_out):
                pe.wait_ge(k_loaded[b], i * 32 + 32)

                def turn_keys(h):
                    if later(s) or h >= 2:
                        pe.wait_ge(kt_evac[h % 2], s * 3 + h // 2)
                    for j in range(4):
                        last = nc.tensor.transpose(ktp[h % 2][:, j * P:(j + 1) * P], kc[b][:, j, h * P:(h + 1) * P], ident[:])
                    last.then_inc(kt_filled[h % 2], 1)
                turn_keys(0)
                turn_keys(1)
                pe.wait_ge(qb_ready, s * 2 + 2)
                if later(s):
                    pe.wait_ge(sm_done, s)
                for h in range(PAIRS):
                    if h == 1:
                        if later(s):
                            pe.wait_ge(kn_evac, s)
                        else:
                            pe.wait_ge(un_evac, 2)
                        if later(i):
                            pe.wait_ge(o_evac, s * 2 - 2)
                    if h + 2 < PAIRS:
                        turn_keys(h + 2)
                    if h == 1:
                        for g in range(PAIRS):
                            last = nc.tensor.transpose(xp[:, g * TDEC:(g + 1) * TDEC], kn[b][:, g * P:(g + 1) * P], ident[:TDEC, :TDEC])
                        last.then_inc(kn_filled, 1)
                    if h == 3 and between:
                        between(0)
                    if h == 4 and between:
                        between(1)
                    pe.wait_ge(kt_evac[h % 2], s * 3 + h // 2 + 1)
                    nc.tensor.matmul(scp[:SROWS, 0:PAST], qb[b][:, h * SROWS:(h + 1) * SROWS], kt[b][:, h, 0:PAST],
                                     start=(h == 0), stop=(h == PAIRS - 1))
                pe.wait_ge(kn_evac, s + 1)
                for h in range(PAIRS):
                    last = nc.tensor.matmul(scp[:SROWS, PAST:KEYS], qb[b][:, h * SROWS:(h + 1) * SROWS], kt[b][:, h, PAST:KEYS],
                                            start=(h == 0), stop=(h == PAIRS - 1))
                last.then_inc(sc_done, 1)

            def pv(s, i, b, part):
                if part == 0:
                    pe.wait_ge(pn_done, s + 1)
                    if later(s):
                        pe.wait_ge(pt_evac, s * 2)
                    for j in range(4):
                        nc.tensor.transpose(ptp[:, j * SROWS:(j + 1) * SROWS], s_[b][:, j * P:(j + 1) * P], ident[:SROWS, :SROWS])
                    nc.tensor.transpose(ptp[:TDEC, 4 * SROWS:5 * SROWS], s_[b][:, PAST:KEYS], ident[:SROWS, :SROWS]).then_inc(pt_filled, 1)
                    return
                pe.wait_ge(v_loaded[b], i * 32 + 32)
                pe.wait_ge(pt_evac, s * 2 + 2)
                if later(s):
                    pe.wait_ge(on_act, s)
                    pe.wait_ge(on_dve, s)
                half = ATTW // 2
                for o in range(2):
                    for j in range(5):
                        x, n = (vc[b][:, j, o * half:(o + 1) * half], P) if j < 4 else (vn[b][:, o * half:(o + 1) * half], TDEC)
                        last = nc.tensor.matmul(pvp[o][:SROWS, 0:half], pts[b][:n, j * SROWS:(j + 1) * SROWS], x,
                                                start=(j == 0), stop=(j == 4))
                last.then_inc(pv_done, 1)

            def pick(s, i, b):
                pe.wait_ge(on_act, s + 1)
                pe.wait_ge(on_dve, s + 1)
                if later(s):
                    pe.wait_ge(o_evac, s * 2)
                for h in range(PAIRS):
                    last = nc.tensor.matmul(picked[:, h * 16:(h + 1) * 16], on[:, h * P:(h + 1) * P],
                                            ident[:SROWS, h * 16:(h + 1) * 16], start=True, stop=True)
                last.then_inc(sel_done, 1)
            def mix():
                pe.wait_ge(z_ready, 1)
                for u in range(6):
                    c, (t0, n) = u // 3, MIXES[u % 3]
                    if u >= 2:
                        pe.wait_ge(mix_evac, u - 1)
                    nc.tensor.matmul(ktp[u % 2][:, 0:n], wp[:, c, :], zt[:, c, t0:t0 + n], start=True, stop=True).then_inc(mixed, 1)
            order(pe, kq, pv, lambda s, i, b: None, pick, mix)


LOGITS = GROUPS + EXPERTS


def load_w_out(sp, d, wraw, w_loaded, k):
    sp.dma_start(wraw[k % WB][:], d["w_out"][0, k * P:(k + 1) * P, :]).then_inc(w_loaded[k % WB], 16)


def project_out(nc, d, ident, eps, turn, cats, hid, xfd, h, lg, wraw, w_loaded):
    with ExitStack() as ctx:
        sb, ps, sem = tools(nc, ctx)
        wh, wl = sb("d_wh", [P, KD, D], F32R), sb("d_wl", [P, KD, D], F32R)
        cat = [sb(f"d_cat{b}", [P, KD, P]) for b in range(2)]
        ch = [sb(f"d_ch{b}", [P, KD, P], F32R) for b in range(2)]
        cl = [sb(f"d_cl{b}", [P, KD, P], F32R) for b in range(2)]
        xr = [sb(f"d_x{b}", [P, D]) for b in range(2)]
        xf = [sb(f"d_xf{b}", [P, D]) for b in range(2)]
        xft = sb("d_xft", [P, KD, P])
        junk, gf = sb("d_junk", [P, D]), sb("d_g", [P, D])
        wr, br = sb("d_wr", [P, KD, LOGITS]), sb("d_br", [P, LOGITS])
        ssq, std, rin = ([sb(f"d_{n}{b}", [P, 1]) for b in range(2)] for n in ("ssq", "std", "rin"))
        op = [ps(f"d_op{b}", [P, D]) for b in range(2)]
        xtp = ps("d_xtp", [P, KD, P])
        lgp = ps("d_lgp", [P, 512])
        consts, w_lo = sem("d_consts"), sem("d_w_lo")
        w_hi = sem("d_w_hi")
        loaded = [sem(f"d_loaded{b}") for b in range(2)]
        c_hi, c_lo, out_done, h_done, rooted, inverted, xf_done = (
            sem("d_" + n) for n in ("c_hi", "c_lo", "out", "h", "rooted", "inverted", "xf"))
        turned, t_evac, routed, lg_done = (
            sem("d_" + n) for n in ("turned", "t_evac", "routed", "lg"))
        stored = [sem(f"d_stored{b}") for b in range(2)]
        block = ctx.enter_context(nc.Block())
        catd = hid.rearrange("(k p) t -> p k t", p=P)
        xp = d["x_prompt"].rearrange("a t d -> (a t) d")
        xs = d["x_sample"].rearrange("a t d -> (a t) d")

        def rows(t, n):
            return slice(t * P, t * P + n) if isinstance(t, int) else bass.ds(t * P, n)

        def h_tile(t, n):
            return (h[:n, t:t + 1, :] if isinstance(t, int) else h[:n, bass.ds(t, 1), :]).rearrange("p a c -> p (a c)")

        def of_next(part, t, i, b):
            if not (isinstance(t, int) and t == QT):
                part(t + 1, i + b, 1 - b, SMP if isinstance(t, int) and t == QT - 1 else P)

        @block.sync
        def _(sp):
            for k in range(WB, KD):
                sp.wait_ge(w_lo, k - WB + 1)
                load_w_out(sp, d, wraw, w_loaded, k)

        @block.gpsimd
        def _(pool):
            def load(t, i, b, n):
                if later(i):
                    pool.wait_ge(c_hi, t - 1)
                    pool.wait_ge(c_lo, t - 1)
                    pool.wait_ge(h_done, t - 1)
                    pool.sem_inc(turn, 1)
                if n == P:
                    pool.dma_start(cat[b][:], catd[:, :, rows(t, P)]).then_inc(loaded[b], 16)
                    pool.dma_start(xr[b][:], xp[rows(t, P), :]).then_inc(loaded[b], 16)
                else:
                    pool.dma_start(xr[b][:n, :], xs).then_inc(loaded[b], 16)
            load(0, 0, 0, P)
            load(1, 0, 1, P)
            pool.dma_start(gf[:], d["g_ffn"].partition_broadcast(P).rearrange("p a d -> p (a d)")).then_inc(consts, 16)
            pool.dma_start(br[:, 0:GROUPS], d["b_router_group"].partition_broadcast(P).rearrange("p a g -> p (a g)")).then_inc(consts, 16)
            pool.dma_start(br[:, GROUPS:], d["b_router_expert"].partition_broadcast(P).rearrange("p a g e -> p (a g e)")).then_inc(consts, 16)
            pool.dma_start(wr[:, :, 0:GROUPS], d["w_router_group"].rearrange("l (k p) g -> p (l k) g", p=P)).then_inc(consts, 16)
            for g in range(GROUPS):
                pool.dma_start(wr[:, :, GROUPS + g * EPG:GROUPS + (g + 1) * EPG],
                               d["w_router_expert"][0, g, :, :].rearrange("(k p) e -> p k e", p=P)).then_inc(consts, 16)
            with pool.Fori(1, QT // 2) as i:
                for b in range(2):
                    load(i * 2 + b, i, b, P)
            load(QT, QT // 2, 0, SMP)

        @block.scalar
        def _(act):
            def split(t, i, b, n):
                if n == P:
                    act.wait_ge(loaded[b], i * 32 + 32)
                if later(i):
                    act.wait_ge(out_done, t - 1)
                src = cat[b][:] if n == P else cats[:]
                nc.scalar.activation(ch[b][:, :, :n], src, ACT.Copy).then_inc(c_hi, 1)

            def project(t, i, b, n):
                of_next(split, t, i, b)
                if not later(t):
                    norm(t, i, b, n)

            def norm(t, i, b, n):
                act.wait_ge(h_done, t + 1)
                nc.scalar.activation(junk[:n, :], h_tile(t, n), ACT.Square, accum_out=ssq[b][:n, :]).then_inc(rooted, 1)
                act.wait_ge(rooted, t * 2 + 1)
                nc.scalar.activation(std[b][:n, :], ssq[b][:n, :], ACT.Sqrt, bias=eps[:n, :], scale=1.0 / D).then_inc(rooted, 1)

            def router(t, i, b, n):
                act.wait_ge(turned, t + 1)
                if later(t):
                    act.wait_ge(routed, t)
                nc.scalar.activation(xft[:, :, :n], xtp[:, :, :n], ACT.Copy).then_inc(t_evac, 1)
                act.wait_ge(xf_done, t + 1)
                act.sem_inc(turn, 1)
                dst = slice(t * P, t * P + n) if isinstance(t, int) else bass.ds(t * P, n)
                act.dma_start(xfd[dst, :], xf[b][:n, :]).then_inc(stored[b], 16)
                of_next(norm, t, i, b)
            nc.scalar.activation(std[0][:], eps[:], ACT.Sqrt)
            for k in range(KD):
                if k == 2:
                    split(0, 0, 0, P)
                act.wait_ge(w_loaded[k % WB], 16 * (k // WB + 1))
                nc.scalar.activation(wh[:, k, :], wraw[k % WB][:], ACT.Copy).then_inc(w_hi, 1)
            two_stages(act, project, router)
            act.wait_ge(stored[0], (QT // 2 + 1) * 16)
            act.wait_ge(stored[1], QT // 2 * 16)

        @block.vector
        def _(dve):
            nc.vector.memset(lg[:], 0.0)

            def split(t, i, b, n):
                dve.wait_ge(c_hi, t + 1)
                src = cat[b][:] if n == P else cats[:]
                nc.vector.tensor_tensor(cl[b][:, :, :n], src, ch[b][:, :, :n].bitcast(F32), ALU.subtract).then_inc(c_lo, 1)

            def project(t, i, b, n):
                of_next(split, t, i, b)
                dve.wait_ge(loaded[b], i * 32 + (32 if n == P else 16))
                if later(i):
                    dve.wait_ge(stored[b], i * 16)
                dve.wait_ge(out_done, t + 1)
                nc.vector.tensor_tensor(h_tile(t, n), op[b][:n, :], xr[b][:n, :], ALU.add).then_inc(h_done, 1)
                dve.wait_ge(rooted, t * 2 + 2)
                nc.vector.reciprocal(rin[b][:n, :], std[b][:n, :]).then_inc(inverted, 1)
                dve.wait_ge(inverted, t + 1)
                nc.vector.scalar_tensor_tensor(xf[b][:n, :], h_tile(t, n), rin[b][:n, :], gf[:n, :],
                                               ALU.mult, ALU.mult).then_inc(xf_done, 1)

            def router(t, i, b, n):
                dve.wait_ge(routed, t + 1)
                one = slice(t, t + 1) if isinstance(t, int) else bass.ds(t, 1)
                nc.vector.tensor_tensor(lg[:n, one, :].rearrange("p a l -> p (a l)"), lgp[:n, 0:LOGITS], br[:n, :],
                                        ALU.add).then_inc(lg_done, 1)
            for k in range(KD):
                if k == 2:
                    split(0, 0, 0, P)
                dve.wait_ge(w_hi, k + 1)
                nc.vector.tensor_tensor(wl[:, k, :], wraw[k % WB][:], wh[:, k, :].bitcast(F32), ALU.subtract).then_inc(w_lo, 1)
            dve.wait_ge(consts, 16 * (4 + GROUPS))
            two_stages(dve, project, router)

        @block.tensor
        def _(pe):
            def project(t, i, b, n):
                pe.wait_ge(c_lo, t + 1)
                if later(i):
                    pe.wait_ge(h_done, t - 1)
                for k in range(KD):
                    if k == KD // 2 and later(t):
                        turn_tile(t - 1, 1 - b, P)
                    if not later(t):
                        pe.wait_ge(w_lo, k + 1)
                    for j, (x, w) in enumerate(((ch, wh), (cl, wh), (ch, wl))):
                        for o in range(2):
                            cols = slice(512 * o, 512 * o + 512)
                            last = nc.tensor.matmul(op[b][:n, cols], x[b][:, k, :n], w[:, k, cols],
                                                    start=(k == 0 and j == 0), stop=(k == KD - 1 and j == 2))
                last.then_inc(out_done, 1)

            def turn_tile(t, b, n):
                if later(t):
                    pe.wait_ge(t_evac, t)
                pe.wait_ge(xf_done, t + 1)
                for k in range(KD):
                    last = nc.tensor.transpose(xtp[:, k, :n], xf[b][:n, k * P:(k + 1) * P], ident[:n, :n])
                last.then_inc(turned, 1)

            def router(t, i, b, n):
                if isinstance(t, int) and t == QT:
                    turn_tile(t, b, n)
                if later(t):
                    pe.wait_ge(lg_done, t)
                if isinstance(t, int) and t == 0:
                    pe.wait_ge(consts, 16 * (4 + GROUPS))
                pe.wait_ge(t_evac, t + 1)
                for k in range(KD):
                    last = nc.tensor.matmul(lgp[:n, 0:LOGITS], xft[:, k, :n], wr[:, k, :], start=(k == 0), stop=(k == KD - 1))
                last.then_inc(routed, 1)
            two_stages(pe, project, router)


def route(nc, d, small, lg, gates, slot, jobs, lst, gfin, gfin_loaded, ins):
    with ExitStack() as ctx:
        sb, ps, sem = tools(nc, ctx)
        tri, ones = sb("e_tri", [P, P]), sb("e_ones", [P, P])
        before = sb("e_before", [P, EXPERTS, EXPERTS])
        tokid = sb("e_tokid", [P, NT], I32)
        gl8, mx8, ix8 = sb("e_gl8", [P, NT, 8]), sb("e_mx8", [P, NT, 8]), sb("e_ix8", [P, NT, 8], U32)
        el8, me8, ie8 = sb("e_el8", [P, NT, 8]), sb("e_me8", [P, NT, 8]), sb("e_ie8", [P, NT, 8], U32)
        g1, i1, i2 = sb("e_g1", [P, NT]), sb("e_i1", [P, NT]), sb("e_i2", [P, NT])
        ex, sm, dv, r = sb("e_ex", [P, NT, GROUPS]), sb("e_sm", [P, NT]), sb("e_dv", [P, NT]), sb("e_r", [P, NT])
        oh, pr = sb("e_oh", [P, NT, GROUPS]), sb("e_pr", [P, NT, GROUPS, EPG])
        ea = [sb(f"e_ea{n}", [P, NT]) for n in range(2)]
        sel = [sb(f"e_sel{n}", [P, NT, EXPERTS]) for n in range(2)]
        m, mp = sb("e_m", [P, NT, EXPERTS]), sb("e_mp", [P, NT + 1, EXPERTS])
        pos, over, base = sb("e_pos", [P, NT, EXPERTS]), sb("e_over", [P, NT, EXPERTS]), sb("e_base", [P, EXPERTS])
        cnt, st, nt = sb("e_cnt", [P, EXPERTS]), sb("e_st", [P, EXPERTS, 11]), sb("e_nt", [P, EXPERTS])
        bm, ob, oi = sb("e_bm", [P, EXPERTS, EXPERTS]), sb("e_ob", [P, EXPERTS]), sb("e_oi", [P, EXPERTS])
        sl, sf = sb("e_sl", [P, NT, EXPERTS]), sb("e_sf", [P, NT])
        jm, jf = sb("e_jm", [1, JOBS, EXPERTS]), sb("e_jf", [1, JOBS + 1])
        pp = ps("e_pp", [P, 512])
        consts, chain, exped, picked, counted, scattered, slots_ready = (
            sem("e_" + n) for n in ("consts", "chain", "exped", "picked", "counted", "scattered", "slots"))
        block = ctx.enter_context(nc.Block())
        V = nc.vector

        def bc(ap, shape):
            return ap.to_broadcast(shape)

        @block.sync
        def _(sp):
            sp.dma_start(tri[:], d["c_tri"]).then_inc(consts, 16)
            sp.dma_start(before[:], d["c_before"].rearrange("p (e f) -> p e f", f=EXPERTS)).then_inc(consts, 16)
            sp.dma_start(tokid[:], d["c_tokid"]).then_inc(consts, 16)
            for r in range(RING):
                load_gate_up(sp, d, ins, r, r)
                load_down(sp, d, ins, r, r)
            sp.dma_start(gfin[:], d["g_final"].partition_broadcast(P)).then_inc(gfin_loaded, 16)

        exp_in = sem("e_exp_in")

        @block.scalar
        def _(act):
            act.wait_ge(exp_in, 1)
            nc.scalar.activation(ex[:], ex[:], ACT.Exp).then_inc(exped, 1)
            act.wait_ge(exp_in, 2)
            nc.scalar.activation(r[:], dv[:], ACT.Exp).then_inc(exped, 1)

        @block.vector
        def _(dve):
            n = [0]

            def link(ins):
                n[0] += 1
                ins.then_inc(chain, 1)
                dve.wait_ge(chain, n[0])

            def col(off, w):
                return small[:, off:off + w]
            V.memset(ones[:], 1.0)
            link(V.memset(gl8[:], -BIG))
            link(V.tensor_copy(gl8[:, :, 0:GROUPS], lg[:, :, 0:GROUPS]))
            for t in range(NT):
                last = V.max(mx8[:, t, :], gl8[:, t, :])
            link(last)
            for t in range(NT):
                last = V.max_index(ix8[:, t, :], mx8[:, t, :], gl8[:, t, :])
            link(last)
            link(V.tensor_copy(g1[:], ix8[:, :, 0]))
            link(V.tensor_tensor(oh[:], bc(g1[:].unsqueeze(2), [P, NT, GROUPS]),
                                 bc(col(C_IOTA, GROUPS).unsqueeze(1), [P, NT, GROUPS]), ALU.is_equal))
            V.tensor_tensor(ex[:], lg[:, :, 0:GROUPS], bc(mx8[:, :, 0:1], [P, NT, GROUPS]), ALU.subtract).then_inc(exp_in, 1)
            link(V.tensor_tensor(pr[:], lg[:, :, GROUPS:].rearrange("p t (g e) -> p t g e", e=EPG),
                                 bc(oh[:].unsqueeze(3), [P, NT, GROUPS, EPG]), ALU.mult))
            link(V.tensor_reduce(el8[:], pr[:].rearrange("p t g e -> p t e g"), AX.X, ALU.add))
            for t in range(NT):
                last = V.max(me8[:, t, :], el8[:, t, :])
            link(last)
            for t in range(NT):
                last = V.max_index(ie8[:, t, :], me8[:, t, :], el8[:, t, :])
            link(last)
            V.tensor_tensor(dv[:], me8[:, :, 1], me8[:, :, 0], ALU.subtract).then_inc(exp_in, 1)
            link(V.tensor_copy(i1[:], ie8[:, :, 0]))
            link(V.tensor_copy(i2[:], ie8[:, :, 1]))
            for a, i in ((0, i1), (1, i2)):
                link(V.scalar_tensor_tensor(ea[a][:], g1[:], float(EPG), i[:], ALU.mult, ALU.add))
                link(V.tensor_tensor(sel[a][:], bc(ea[a][:].unsqueeze(2), [P, NT, EXPERTS]),
                                     bc(col(C_EXP, EXPERTS).unsqueeze(1), [P, NT, EXPERTS]), ALU.is_equal))
            link(V.tensor_tensor(m[:], sel[0][:], sel[1][:], ALU.add))
            link(V.memset(m[SMP:, QT, :], 0.0))
            link(V.memset(mp[:, 0, :], 0.0))
            for t in range(NT):
                link(V.tensor_tensor(mp[:, t + 1, :], mp[:, t, :], m[:, t, :], ALU.add))
            dve.sem_inc(picked, 1)
            dve.wait_ge(exped, 2)
            link(V.tensor_reduce(sm[:], ex[:], AX.X, ALU.add))
            link(V.scalar_tensor_tensor(sm[:], r[:], 1.0, sm[:], ALU.add, ALU.mult))
            link(V.reciprocal(gates[:, 0, :], sm[:]))
            link(V.tensor_tensor(gates[:, 1, :], gates[:, 0, :], r[:], ALU.mult))
            dve.wait_ge(counted, 1)
            link(V.tensor_copy(pos[:], pp[:, 0:NT * EXPERTS].rearrange("p (t e) -> p t e", e=EXPERTS)))
            link(V.tensor_copy(cnt[:], pp[:, NT * EXPERTS:(NT + 1) * EXPERTS]))
            link(V.tensor_tensor(st[:], bc(cnt[:].unsqueeze(2), [P, EXPERTS, 11]),
                                 bc(col(C_STEP, 11).unsqueeze(1), [P, EXPERTS, 11]), ALU.is_gt))
            link(V.tensor_reduce(nt[:], st[:], AX.X, ALU.add))
            link(V.tensor_tensor(bm[:], before[:], bc(nt[:].unsqueeze(1), [P, EXPERTS, EXPERTS]), ALU.mult))
            link(V.tensor_reduce(ob[:], bm[:], AX.X, ALU.add))
            link(V.tensor_tensor(oi[:], ob[:], nt[:], ALU.add))
            link(V.scalar_tensor_tensor(base[:], ob[:], float(EXPERTS - 1), col(C_EXP, EXPERTS), ALU.add, ALU.subtract))
            link(V.tensor_scalar(over[:], pos[:], float(CAP), None, ALU.is_ge))
            link(V.tensor_tensor(over[:], over[:], bc(base[:].unsqueeze(1), [P, NT, EXPERTS]), ALU.mult))
            link(V.tensor_tensor(over[:], over[:], bc(col(C_EXP, EXPERTS).unsqueeze(1), [P, NT, EXPERTS]), ALU.add))
            link(V.scalar_tensor_tensor(pos[:], over[:], float(CAP), pos[:], ALU.mult, ALU.add))
            for a in range(2):
                link(V.tensor_tensor(sl[:], sel[a][:], pos[:], ALU.mult))
                link(V.tensor_reduce(sf[:], sl[:], AX.X, ALU.add))
                link(V.tensor_copy(slot[:, a, :], sf[:]))
                dve.sem_inc(slots_ready, 1)
            link(V.tensor_tensor(jm[:], bc(small[0:1, C_JOB:C_JOB + JOBS].unsqueeze(2), [1, JOBS, EXPERTS]),
                                 bc(oi[0:1, :].unsqueeze(1), [1, JOBS, EXPERTS]), ALU.is_ge))
            link(V.tensor_reduce(jf[:, 0:JOBS], jm[:], AX.X, ALU.add))
            link(V.tensor_scalar(jf[:, 0:JOBS], jf[:, 0:JOBS], float(EXPERTS - 1), None, ALU.min))
            link(V.tensor_copy(jf[:, 0:EXPERTS], small[0:1, C_EXP:C_EXP + EXPERTS]))
            link(V.tensor_scalar(jm[:, 0, 0:EXPERTS], small[0:1, C_EXP:C_EXP + EXPERTS], float(RING), oi[0:1, EXPERTS - 1:EXPERTS],
                                 ALU.mult, ALU.is_lt))
            link(V.tensor_reduce(jf[:, JOBS:JOBS + 1], jm[:, 0, 0:EXPERTS], AX.X, ALU.add))
            link(V.tensor_scalar(jf[:, JOBS:JOBS + 1], jf[:, JOBS:JOBS + 1], float(EXPERTS // RING - 1), None, ALU.add))
            link(V.tensor_copy(jobs[0:1, :], jf[:]))

        @block.tensor
        def _(pe):
            pe.wait_ge(consts, 48)
            pe.wait_ge(picked, 1)
            w = NT * EXPERTS
            nc.tensor.matmul(pp[:, 0:w], tri[:], m[:].rearrange("p t e -> p (t e)"), start=True, stop=False)
            nc.tensor.matmul(pp[:, 0:w], ones[:], mp[:, 0:NT, :].rearrange("p t e -> p (t e)"), start=False, stop=True)
            nc.tensor.matmul(pp[:, w:w + EXPERTS], ones[:], mp[:, NT, :], start=True, stop=True).then_inc(counted, 1)

        @block.gpsimd
        def _(pool):
            pool.wait_ge(consts, 48)
            for a in range(2):
                pool.wait_ge(slots_ready, a + 1)
                for t in range(NT):
                    n = P if t < QT else SMP
                    pool.indirect_dma_start(out=lst, out_offset=bass.IndirectOffsetOnAxis(ap=slot[:n, a, t:t + 1].bitcast(U32), axis=0),
                                            in_=tokid[:n, t:t + 1], in_offset=None).then_inc(scattered, 16)
            pool.wait_ge(scattered, NT * 32)


def experts(nc, d, ident, turn, jobs, lst, xfd, yb, ins):
    with ExitStack() as ctx:
        sb, ps, sem = tools(nc, ctx)
        wg, wu, wd, xg = ins.wg, ins.wu, ins.wd, ins.xg
        idx0, idx0_loaded = sb("f_idx_first", [CAP, RING], I32), sem("f_idx_first_loaded")
        xt = [sb(f"f_xt{b}", [P, KD, CAP]) for b in range(2)]
        sg = [sb(f"f_sg{b}", [P, 2, CAP]) for b in range(2)]
        ht = [sb(f"f_ht{b}", [P, 2, CAP]) for b in range(2)]
        hh, hl = ([sb(f"f_{n}{b}", [P, 2, CAP], F32R) for b in range(2)] for n in ("hh", "hl"))
        wdh, wdl = sb("f_wdh", [P, 2, D], F32R), sb("f_wdl", [P, 2, D], F32R)
        y = [sb(f"f_y{b}", [CAP, D]) for b in range(2)]
        xtp = [ps(f"f_xtp{b}", [P, 4, P]) for b in range(2)]
        gp, upp = ps("f_gp", [P, 4, P]), ps("f_up", [P, 4, P])
        yp = [ps(f"f_yp{b}", [P, 512]) for b in range(2)]
        w_loaded, wd_loaded, gathered = ins.w_loaded, ins.wd_loaded, ins.gathered
        turned, t_act, t_dve = sem("f_turned"), sem("f_t_act"), sem("f_t_dve")
        up_done, silu_done, h_mult, h_done, wd_hi, wd_lo, down_done, y_act, y_dve = (
            sem("f_" + n) for n in ("up", "silu", "h_mult", "h", "wd_hi", "wd_lo", "down", "y_act", "y_dve"))
        stored = [sem(f"f_stored{b}") for b in range(2)]
        block = ctx.enter_context(nc.Block())
        most = JOBS // RING

        def turns(eng):
            return eng.value_load(jobs[0:1, JOBS:JOBS + 1], min_val=EXPERTS // RING - 1, max_val=most - 1)

        def order(eng, gather, up, down, split):
            i_last = turns(eng)
            gather(0, 0, 0)
            up(0, 0, 0)
            gather(1, 0, 1)
            split(0, 0, 0)
            with eng.Fori(0, i_last) as i:
                for r in range(1, RING + 1):
                    up(i * RING + r, i + r // RING, r % RING)
                    gather(i * RING + (r + 1), i + (r + 1) // RING, (r + 1) % RING)
                    down(i * RING + (r - 1), i, r - 1)
                    split(i * RING + r, i + r // RING, r % RING)
            i = i_last
            for r in range(1, RING):
                up(i * RING + r, i, r)
                if r + 1 < RING:
                    gather(i * RING + (r + 1), i, r + 1)
                down(i * RING + (r - 1), i, r - 1)
                split(i * RING + r, i, r)
            down(i * RING + (RING - 1), i, RING - 1)

        @block.sync
        def _(sp):
            i_last = turns(sp)

            with sp.Fori(0, i_last) as i:
                for r in range(RING):
                    e = sp.value_load(jobs[0:1, bass.ds(i * RING + (RING + r), 1)], min_val=0, max_val=EXPERTS - 1)
                    sp.wait_ge(up_done, i * RING + r + 1)
                    sp.sem_inc(turn, 1)
                    load_gate_up(sp, d, ins, e, r)
                    sp.wait_ge(wd_lo, i * RING + r + 1)
                    sp.sem_inc(turn, 1)
                    load_down(sp, d, ins, e, r)

        @block.gpsimd
        def _(pool):
            i_last = turns(pool)

            first = lst[0:RING * CAP, :].rearrange("(r p) a -> p (r a)", p=CAP)
            pool.dma_start(idx0[:], first, allow_slow_non_contiguous=True).then_inc(idx0_loaded, 16)
            pool.wait_ge(idx0_loaded, 16)
            for r in range(RING):
                gather_tokens(pool, ins, xfd, idx0[:, r:r + 1], r)
            for r in range(2):
                load_list(pool, ins, lst, RING + r, r)
            with pool.Fori(1, i_last + 1) as i:
                for r in range(RING):
                    ahead, turn_ahead = (r + 2) % RING, i + (r + 2) // RING
                    pool.wait_ge(ins.gathered[ahead], turn_ahead * 16)
                    pool.sem_inc(turn, 1)
                    load_list(pool, ins, lst, i * RING + (r + 2), ahead)
                    pool.wait_ge(turned, i * RING + (r - RING + 1))
                    pool.wait_ge(ins.idx_loaded[r], i * 16)
                    pool.sem_inc(turn, 1)
                    gather_tokens(pool, ins, xfd, ins.idx[r][:], r)
            for r in range(2):
                pool.wait_ge(ins.idx_loaded[r], i_last * 16 + 16)
                pool.sem_inc(turn, 1)

        @block.scalar
        def _(act):
            def gather(j, i, r):
                act.wait_ge(turned, j + 1)
                nc.scalar.activation(xt[r % 2][:, 0:4, :], xtp[0][:, :, 0:CAP], ACT.Copy).then_inc(t_act, 1)

            def up(j, i, r):
                act.wait_ge(up_done, j + 1)
                nc.scalar.activation(sg[r % 2][:], gp[:, 0:2, 0:CAP], ACT.Silu).then_inc(silu_done, 1)

            def down(j, i, r):
                act.wait_ge(stored[r % 2], i * 32 + (r // 2) * 16 + 1)
                act.wait_ge(down_done, j + 1)
                nc.scalar.activation(y[r % 2][:, 0:512], yp[0][:CAP, :], ACT.Copy).then_inc(y_act, 1)
                act.wait_ge(y_act, j + 2)
                act.wait_ge(y_dve, j + 2)
                act.sem_inc(turn, 1)
                act.dma_start(yb[bass.ds(j * CAP, CAP), :], y[r % 2][:]).then_inc(stored[r % 2], 16)

            def split(j, i, r):
                act.wait_ge(wd_loaded[r], i * 16 + 16)
                nc.scalar.activation(wdh[:], wd[r][:], ACT.Copy).then_inc(wd_hi, 1)
            nc.scalar.activation(sg[0][:, 0, 0:1], ident[:, 0:1], ACT.Silu)
            order(act, gather, up, down, split)
            i_last = turns(act)
            for b in range(2):
                act.wait_ge(stored[b], i_last * 32 + 33)
                act.sem_inc(turn, 1)

        @block.vector
        def _(dve):
            dve.sem_inc(stored[0], 1)
            dve.sem_inc(stored[1], 1)
            dve.sem_inc(y_dve, 1)
            dve.sem_inc(y_act, 1)

            def gather(j, i, r):
                dve.wait_ge(turned, j + 1)
                nc.vector.tensor_copy(xt[r % 2][:, 4:8, :], xtp[1][:, :, 0:CAP]).then_inc(t_dve, 1)

            def up(j, i, r):
                dve.wait_ge(silu_done, j + 1)
                nc.vector.tensor_tensor(ht[r % 2][:], sg[r % 2][:], upp[:, 0:2, 0:CAP], ALU.mult)
                nc.vector.tensor_tensor(hh[r % 2][:], sg[r % 2][:], upp[:, 0:2, 0:CAP], ALU.mult).then_inc(h_mult, 1)
                dve.wait_ge(h_mult, j + 1)
                nc.vector.tensor_tensor(hl[r % 2][:], ht[r % 2][:], hh[r % 2][:].bitcast(F32), ALU.subtract).then_inc(h_done, 1)

            def down(j, i, r):
                dve.wait_ge(stored[r % 2], i * 32 + (r // 2) * 16 + 1)
                dve.wait_ge(down_done, j + 1)
                nc.vector.tensor_copy(y[r % 2][:, 512:D], yp[1][:CAP, :]).then_inc(y_dve, 1)

            def split(j, i, r):
                dve.wait_ge(wd_hi, j + 1)
                nc.vector.tensor_tensor(wdl[:], wd[r][:], wdh[:].bitcast(F32), ALU.subtract).then_inc(wd_lo, 1)
            order(dve, gather, up, down, split)

        @block.tensor
        def _(pe):
            def gather(j, i, r):
                pe.wait_ge(gathered[r], i * 16 + 16)
                if not isinstance(j, int) or j >= 1:
                    pe.wait_ge(t_act, j)
                    pe.wait_ge(t_dve, j)
                rows = xg[r][:].rearrange("t (p k) -> t k p", k=KD)
                for k in range(KD):
                    last = nc.tensor.transpose(xtp[k // 4][:, k % 4, 0:CAP], rows[:, k, :], ident[:CAP, :CAP])
                last.then_inc(turned, 1)

            def up(j, i, r):
                pe.wait_ge(w_loaded[r], i * 32 + 32)
                pe.wait_ge(t_act, j + 1)
                pe.wait_ge(t_dve, j + 1)
                if not isinstance(j, int) or j >= 1:
                    pe.wait_ge(h_done, j)
                for w, dst in ((wg, gp), (wu, upp)):
                    cols = w[r][:].rearrange("p k (m c) -> p k c m", c=2)
                    for c in range(2):
                        for k in range(KD):
                            last = nc.tensor.matmul(dst[:, c, 0:CAP], cols[:, k, c, :], xt[r % 2][:, k, :],
                                                    start=(k == 0), stop=(k == KD - 1))
                last.then_inc(up_done, 1)

            def down(j, i, r):
                pe.wait_ge(h_done, j + 1)
                pe.wait_ge(wd_lo, j + 1)
                pe.wait_ge(y_act, j + 1)
                pe.wait_ge(y_dve, j + 1)
                for o in range(2):
                    for c in range(2):
                        for q, (x, w) in enumerate(((hh, wdh), (hl, wdh), (hh, wdl))):
                            last = nc.tensor.matmul(yp[o][:CAP, :], x[r % 2][:, c, :], w[:, c, 512 * o:512 * o + 512],
                                                    start=(c == 0 and q == 0), stop=(c == 1 and q == 2))
                last.then_inc(down_done, 1)
            order(pe, gather, up, down, lambda j, i, r: None)


def combine(nc, d, eps, h, gates, slot, yb, gfin, gfin_loaded):
    with ExitStack() as ctx:
        sb, ps, sem = tools(nc, ctx)
        B = 4
        ya = [[sb(f"g_y{a}{b}", [P, D]) for b in range(B)] for a in range(2)]
        s1, s2, out = ([sb(f"g_{n}{b}", [P, D]) for b in range(B)] for n in ("s1", "s2", "o"))
        junk = sb("g_junk", [P, D])
        ssq, std, rin = ([sb(f"g_{n}{b}", [P, 1]) for b in range(B)] for n in ("ssq", "std", "rin"))
        y_loaded = [sem(f"g_y_loaded{b}") for b in range(B)]
        added, summed, rooted, inverted, normed = (sem("g_" + n) for n in ("added", "summed", "rooted", "inverted", "normed"))
        stored = [sem(f"g_stored{b}") for b in range(B)]
        block = ctx.enter_context(nc.Block())
        yp = d["o_y_prompt"].rearrange("a t d -> (a t) d")
        ys = d["o_y_sample"].rearrange("a t d -> (a t) d")
        N = [P] * QT + [SMP]

        @block.gpsimd
        def _(pool):
            for t, n in enumerate(N):
                if t >= B:
                    pool.wait_ge(summed, t - B + 1)
                for a in range(2):
                    pool.indirect_dma_start(out=ya[a][t % B][:n, :], out_offset=None, in_=yb,
                                            in_offset=bass.IndirectOffsetOnAxis(ap=slot[:n, a, t:t + 1].bitcast(U32), axis=0)
                                            ).then_inc(y_loaded[t % B], 16)

        @block.sync
        def _(sp):
            for t, n in enumerate(N):
                sp.wait_ge(normed, t + 1)
                dst = yp[t * P:(t + 1) * P, :] if t < QT else ys
                sp.dma_start(dst, out[t % B][:n, :]).then_inc(stored[t % B], 16)
            for b in range(B):
                sp.wait_ge(stored[b], len(range(b, NT, B)) * 16)

        @block.scalar
        def _(act):
            nc.scalar.activation(std[0][:], eps[:], ACT.Sqrt)
            for t, n in enumerate(N):
                b = t % B
                act.wait_ge(summed, t + 1)
                nc.scalar.activation(junk[:n, :], s2[b][:n, :], ACT.Square, accum_out=ssq[b][:n, :]).then_inc(rooted, 1)
                act.wait_ge(rooted, 2 * t + 1)
                nc.scalar.activation(std[b][:n, :], ssq[b][:n, :], ACT.Sqrt, bias=eps[:n, :], scale=1.0 / D).then_inc(rooted, 1)

        @block.vector
        def _(dve):
            dve.wait_ge(gfin_loaded, 16)

            def total(t):
                n, b = N[t], t % B
                dve.wait_ge(y_loaded[b], 32 * (t // B + 1))
                nc.vector.scalar_tensor_tensor(s1[b][:n, :], ya[0][b][:n, :], gates[:n, 0, t:t + 1], h[:n, t, :],
                                               ALU.mult, ALU.add).then_inc(added, 1)
                dve.wait_ge(added, t + 1)
                nc.vector.scalar_tensor_tensor(s2[b][:n, :], ya[1][b][:n, :], gates[:n, 1, t:t + 1], s1[b][:n, :],
                                               ALU.mult, ALU.add).then_inc(summed, 1)

            def norm(t):
                n, b = N[t], t % B
                dve.wait_ge(rooted, 2 * t + 2)
                nc.vector.reciprocal(rin[b][:n, :], std[b][:n, :]).then_inc(inverted, 1)
                dve.wait_ge(inverted, t + 1)
                if t >= B:
                    dve.wait_ge(stored[b], 16 * (t // B))
                nc.vector.scalar_tensor_tensor(out[b][:n, :], s2[b][:n, :], rin[b][:n, :], gfin[:n, :],
                                               ALU.mult, ALU.mult).then_inc(normed, 1)
            total(0)
            for t in range(1, NT):
                total(t)
                norm(t - 1)
            norm(NT - 1)


_INS = ['x_prompt', 'x_sample', 'cache_k', 'cache_v', 'state_pool', 'g_mix', 'w_in', 'w_pool', 'pool_scale', 'w_out',
        'g_ffn', 'w_router_group', 'b_router_group', 'w_router_expert', 'b_router_expert', 'w_gate', 'w_up', 'w_down',
        'g_final']
_OUTS = [('o_y_prompt', (1, SEQ, D)), ('o_y_sample', (NSEQ, TDEC, D)),
         ('o_k_prompt', (1, 1, SEQ, HEADS, HD)), ('o_v_prompt', (1, 1, SEQ, HEADS, HD)),
         ('o_pool_prompt', (1, 1, POOL_STATE, POOLW)),
         ('o_k_sample', (1, NSEQ, TDEC, HEADS, HD)), ('o_v_sample', (1, NSEQ, TDEC, HEADS, HD)),
         ('o_pool_sample', (1, NSEQ, POOL_STATE, POOLW))]


def kernel(**inputs):
    import concourse.bacc as _bacc
    from concourse.bass_utils import run_bass_kernel_spmd as _run

    nc = _bacc.Bacc("TRN2", target_bir_lowering=False, num_devices=1)
    arrays, d = {}, {}
    for name, a in [(n, np.ascontiguousarray(inputs[n])) for n in _INS] + list(constants().items()):
        arrays[f"in_{name}"] = a
        d[name] = nc.dram_tensor(f"in_{name}", a.shape, mybir.dt.from_np(a.dtype), kind="ExternalInput").ap()
    for name, shape in _OUTS:
        d[name] = nc.dram_tensor(name, shape, F32, kind="ExternalOutput").ap()
    build(nc, d)
    r = _run(nc, [arrays], core_ids=[0])
    return tuple(r.results[0][name] for name, _ in _OUTS)
```
